# Optimizing a Trainium2 kernel written in Bass

```python
import math
import jax
import jax.numpy as jnp
from jax import lax
import numpy as np

D_MODEL = 1024
BATCH = 1
SEQ = 512
DEPTH = 2

HEAD_DIM = 64
ROPE_THETA = 10000.0
A_HEADS = D_MODEL // (2 * HEAD_DIM)
A_BRANCHES = ((128, 1), (512, 4), (2048, 16))
B_HEADS = D_MODEL // (4 * HEAD_DIM)
B_VDIM = 2 * HEAD_DIM
A_WIDTH = A_HEADS * HEAD_DIM
B_WIDTH = B_HEADS * 2 * HEAD_DIM
EVEN_IN = 3 * A_WIDTH + 3 * B_WIDTH
Q_BLOCK = 128
C_HEADS = D_MODEL // 128
C_DK = 128
C_DV = 128
C_WIDTH = C_HEADS * C_DV
CONV_W = 4
CHUNK = 64
ODD_IN = 4 * C_WIDTH + 2 * C_HEADS
N_GROUPS = 4
EXPERTS_PER_GROUP = 8
N_EXPERTS = N_GROUPS * EXPERTS_PER_GROUP
TOP_K = 2
EXPERT_FF = D_MODEL // 2
MOE_BLOCK = 128
EPS = 1e-6
NEG_INF = -1e30

kernel_name = 'hybrid_dilated_diffattn_gdn_hmoe'

def rms_norm(x, gain):
    xf = x.astype(jnp.float32)
    y = xf * lax.rsqrt(jnp.mean(xf * xf, axis=-1, keepdims=True) + EPS)
    return (y * gain.astype(jnp.float32)).astype(x.dtype)

def rope_tables(seq_len, dim):
    inv_freq = 1.0 / (ROPE_THETA ** (jnp.arange(0, dim, 2, dtype=jnp.float32) / dim))
    ang = jnp.arange(seq_len, dtype=jnp.float32)[:, None] * inv_freq[None, :]
    return jnp.cos(ang), jnp.sin(ang)

def apply_rope(x, cos, sin):
    xf = x.astype(jnp.float32)
    x1, x2 = jnp.split(xf, 2, axis=-1)
    c = cos[None, :, None, :]
    s = sin[None, :, None, :]
    return jnp.concatenate([x1 * c - x2 * s, x2 * c + x1 * s], axis=-1).astype(x.dtype)

def qk_norm_rope(t, gain, cos, sin):
    return apply_rope(rms_norm(t, gain), cos, sin)

def dilated_branch(q, k, v, window, dilation):
    B, S, H, hd = q.shape
    n = window // dilation
    L = S // dilation
    nb = -(-L // n)
    Lp = nb * n

    def to_residue(t):
        t = t.reshape(B, L, dilation, H, hd).transpose(0, 2, 1, 3, 4)
        return jnp.pad(t, ((0, 0), (0, 0), (0, Lp - L), (0, 0), (0, 0)))

    def band(t):
        tp = jnp.pad(t, ((0, 0), (0, 0), (n, 0), (0, 0), (0, 0))).reshape(B, dilation, nb + 1, n, H, hd)
        return jnp.concatenate([tp[:, :, :-1], tp[:, :, 1:]], axis=3)

    qb = to_residue(q).reshape(B, dilation, nb, n, H, hd)
    kb = band(to_residue(k))
    vb = band(to_residue(v))
    s = jnp.einsum('brcihd,brcjhd->brchij', qb, kb).astype(jnp.float32) * (hd ** -0.5)
    i = jnp.arange(n)[:, None]
    j = jnp.arange(2 * n)[None, :]
    blk = jnp.arange(nb)[:, None, None]
    dist = n + i - j
    mask = (dist >= 0) & (dist <= n) & (blk * n + j >= n)
    s = jnp.where(mask[None, None, :, None], s, NEG_INF)
    m = jnp.max(s, axis=-1, keepdims=True)
    p = jnp.exp(s - m)
    den = jnp.sum(p, axis=-1)
    o = jnp.einsum('brchij,brcjhd->brcihd', p, vb.astype(jnp.float32))
    o = o / jnp.moveaxis(den, -1, 3)[..., None]
    lse = jnp.moveaxis(m[..., 0] + jnp.log(den), -1, 3)
    o = o.reshape(B, dilation, Lp, H, hd)[:, :, :L].transpose(0, 2, 1, 3, 4).reshape(B, S, H, hd)
    lse = lse.reshape(B, dilation, Lp, H)[:, :, :L].transpose(0, 2, 1, 3).reshape(B, S, H)
    return o, lse

def dilated_attention(q, k, v):
    outs, lses = [], []
    for window, dilation in A_BRANCHES:
        o, lse = dilated_branch(q, k, v, window, dilation)
        outs.append(o)
        lses.append(lse)
    wts = jax.nn.softmax(jnp.stack(lses, 0), axis=0)
    return jnp.einsum('gbsh,gbshd->bshd', wts, jnp.stack(outs, 0))

def diff_attention(q, k, v, lam, lam_init, out_gain):
    B, S, H, _, hd = q.shape
    scale = hd ** -0.5
    outs = []
    for blk in range(S // Q_BLOCK):
        lo, hi = blk * Q_BLOCK, (blk + 1) * Q_BLOCK
        s = jnp.einsum('bihcd,bjhcd->bhcij', q[:, lo:hi], k[:, :hi]).astype(jnp.float32) * scale
        causal = (lo + jnp.arange(Q_BLOCK))[:, None] >= jnp.arange(hi)[None, :]
        p = jax.nn.softmax(jnp.where(causal, s, NEG_INF), axis=-1)
        a = p[:, :, 0] - lam[None, :, None, None] * p[:, :, 1]
        outs.append(jnp.einsum('bhij,bjhe->bihe', a, v[:, :hi].astype(jnp.float32)))
    o = jnp.concatenate(outs, axis=1)
    return rms_norm(o, out_gain) * (1.0 - lam_init)

def even_mixer(h, w_in, a_q_gain, a_k_gain, b_q_gain, b_k_gain, lq1, lk1, lq2, lk2, b_out_gain, w_out,
               lam_init, cos, sin):
    B, S, _ = h.shape
    proj = h @ w_in
    cuts = [A_WIDTH, 2 * A_WIDTH, 3 * A_WIDTH, 3 * A_WIDTH + B_WIDTH, 3 * A_WIDTH + 2 * B_WIDTH]
    aq, ak, av, bq, bk, bv = jnp.split(proj, cuts, axis=-1)
    aq = qk_norm_rope(aq.reshape(B, S, A_HEADS, HEAD_DIM), a_q_gain, cos, sin)
    ak = qk_norm_rope(ak.reshape(B, S, A_HEADS, HEAD_DIM), a_k_gain, cos, sin)
    av = av.reshape(B, S, A_HEADS, HEAD_DIM)
    oa = dilated_attention(aq, ak, av).reshape(B, S, A_WIDTH)
    bq = qk_norm_rope(bq.reshape(B, S, 2 * B_HEADS, HEAD_DIM), b_q_gain, cos, sin).reshape(B, S, B_HEADS, 2, HEAD_DIM)
    bk = qk_norm_rope(bk.reshape(B, S, 2 * B_HEADS, HEAD_DIM), b_k_gain, cos, sin).reshape(B, S, B_HEADS, 2, HEAD_DIM)
    bv = bv.reshape(B, S, B_HEADS, B_VDIM)
    f32 = jnp.float32
    lam = (jnp.exp(jnp.sum(lq1.astype(f32) * lk1.astype(f32), -1))
           - jnp.exp(jnp.sum(lq2.astype(f32) * lk2.astype(f32), -1)) + lam_init)
    ob = diff_attention(bq, bk, bv, lam, lam_init, b_out_gain).reshape(B, S, B_WIDTH)
    return jnp.concatenate([oa, ob], axis=-1).astype(h.dtype) @ w_out

def causal_depthwise_conv(x, w):
    return lax.conv_general_dilated(x, w[:, None, :].astype(x.dtype), window_strides=(1,),
                                    padding=((w.shape[0] - 1, 0),),
                                    dimension_numbers=('NWC', 'WIO', 'NWC'),
                                    feature_group_count=x.shape[-1])

def l2_normalize(x):
    xf = x.astype(jnp.float32)
    return xf * lax.rsqrt(jnp.sum(xf * xf, axis=-1, keepdims=True) + EPS)

def chunk_gated_delta_rule(q, k, v, g, beta):
    B, S, H, dk = q.shape
    dv = v.shape[-1]
    nc = S // CHUNK
    f32 = jnp.float32

    def chunks(t):
        t = jnp.moveaxis(t.astype(f32), 2, 1)
        return t.reshape(B, H, nc, CHUNK, *t.shape[3:])

    q = chunks(q) * (dk ** -0.5)
    k = chunks(k)
    v = chunks(v)
    beta = chunks(beta)
    g = jnp.cumsum(chunks(g), axis=-1)
    tril = jnp.tril(jnp.ones((CHUNK, CHUNK), bool))
    strict = jnp.tril(jnp.ones((CHUNK, CHUNK), bool), k=-1)
    gdiff = g[..., :, None] - g[..., None, :]
    decay = jnp.where(tril, jnp.exp(jnp.where(tril, gdiff, 0.0)), 0.0)
    k_beta = k * beta[..., None]
    v_beta = v * beta[..., None]
    lmat = jnp.where(strict, jnp.einsum('bhnid,bhnjd->bhnij', k_beta, k) * decay, 0.0)
    eye = jnp.eye(CHUNK, dtype=f32)
    t_inv = lax.linalg.triangular_solve(eye + lmat, jnp.broadcast_to(eye, lmat.shape),
                                        left_side=True, lower=True)
    u = t_inv @ v_beta
    w = t_inv @ (k_beta * jnp.exp(g)[..., None])
    a_intra = jnp.where(tril, jnp.einsum('bhnid,bhnjd->bhnij', q, k) * decay, 0.0)

    def step(state, xs):
        q_c, k_c, u_c, w_c, g_c, a_c = xs
        v_new = u_c - w_c @ state
        o = (q_c * jnp.exp(g_c)[..., None]) @ state + a_c @ v_new
        g_last = g_c[..., -1]
        k_dec = k_c * jnp.exp(g_last[..., None] - g_c)[..., None]
        state = state * jnp.exp(g_last)[..., None, None] + jnp.einsum('bhcd,bhce->bhde', k_dec, v_new)
        return state, o

    xs = (jnp.moveaxis(q, 2, 0), jnp.moveaxis(k, 2, 0), jnp.moveaxis(u, 2, 0),
          jnp.moveaxis(w, 2, 0), jnp.moveaxis(g, 2, 0), jnp.moveaxis(a_intra, 2, 0))
    state0 = jnp.zeros((B, H, dk, dv), f32)
    _, o = lax.scan(step, state0, xs)
    o = jnp.moveaxis(o, 0, 2).reshape(B, H, S, dv)
    return jnp.moveaxis(o, 1, 2)

def odd_mixer(h, w_in, conv_w, a_log, dt_bias, out_gain, w_out):
    B, S, _ = h.shape
    f32 = jnp.float32
    proj = h @ w_in
    qkv = jax.nn.silu(causal_depthwise_conv(proj[..., :3 * C_WIDTH], conv_w))
    q, k, v = jnp.split(qkv, 3, axis=-1)
    z = proj[..., 3 * C_WIDTH:4 * C_WIDTH].reshape(B, S, C_HEADS, C_DV)
    a = proj[..., 4 * C_WIDTH:4 * C_WIDTH + C_HEADS].astype(f32)
    b = proj[..., 4 * C_WIDTH + C_HEADS:].astype(f32)
    q = l2_normalize(q.reshape(B, S, C_HEADS, C_DK))
    k = l2_normalize(k.reshape(B, S, C_HEADS, C_DK))
    v = v.reshape(B, S, C_HEADS, C_DV)
    g = -jnp.exp(a_log.astype(f32)) * jax.nn.softplus(a + dt_bias.astype(f32))
    beta = jax.nn.sigmoid(b)
    o = chunk_gated_delta_rule(q, k, v, g, beta)
    o = rms_norm(o, out_gain) * jax.nn.silu(z.astype(f32))
    return o.reshape(B, S, C_WIDTH).astype(h.dtype) @ w_out

def grouped_expert_ffn(xf, expert_ids, weights, w_gate, w_up, w_down):
    N, D = xf.shape
    E = w_gate.shape[0]
    A = N * TOP_K
    flat_e = expert_ids.reshape(-1).astype(jnp.int32)
    flat_tok = jnp.repeat(jnp.arange(N, dtype=jnp.int32), TOP_K)
    flat_w = weights.reshape(-1).astype(jnp.float32)
    order = jnp.argsort(flat_e)
    se, stok, sw = flat_e[order], flat_tok[order], flat_w[order]
    counts = jnp.bincount(flat_e, length=E)
    padded = (counts + MOE_BLOCK - 1) // MOE_BLOCK * MOE_BLOCK
    pad_end = jnp.cumsum(padded)
    pad_start = pad_end - padded
    seg_start = jnp.cumsum(counts) - counts
    dest = pad_start[se] + (jnp.arange(A, dtype=jnp.int32) - seg_start[se])
    n_blocks = -(-(A + E * (MOE_BLOCK - 1)) // MOE_BLOCK)
    P = n_blocks * MOE_BLOCK
    row_tok = jnp.full((P,), N, jnp.int32).at[dest].set(stok)
    row_w = jnp.zeros((P,), jnp.float32).at[dest].set(sw)
    block_start = jnp.arange(n_blocks, dtype=jnp.int32) * MOE_BLOCK
    block_e = jnp.minimum(jnp.searchsorted(pad_end, block_start, side='right'), E - 1)
    x_pad = jnp.concatenate([xf, jnp.zeros((1, D), xf.dtype)], axis=0)

    def block_ffn(args):
        toks, e = args
        xb = x_pad[toks]
        hb = jax.nn.silu(xb @ w_gate[e]) * (xb @ w_up[e])
        return hb @ w_down[e]

    yb = lax.map(block_ffn, (row_tok.reshape(n_blocks, MOE_BLOCK), block_e))
    y = (yb.reshape(P, D).astype(jnp.float32) * row_w[:, None]).astype(xf.dtype)
    return jnp.zeros((N + 1, D), xf.dtype).at[row_tok].add(y)[:N]

def hier_moe(h, w_group, b_group, w_erouter, b_erouter, w_gate, w_up, w_down):
    B, S, D = h.shape
    f32 = jnp.float32
    xf = h.reshape(B * S, D)
    gl = (xf @ w_group).astype(f32) + b_group.astype(f32)
    grp = jnp.argmax(gl, axis=-1)
    g_w = jnp.max(jax.nn.softmax(gl, axis=-1), axis=-1)
    el = jnp.einsum('nd,gde->nge', xf, w_erouter).astype(f32) + b_erouter.astype(f32)
    el = jnp.einsum('nge,ng->ne', el, jax.nn.one_hot(grp, N_GROUPS, dtype=f32))
    top_v, top_i = lax.top_k(el, TOP_K)
    weights = g_w[:, None] * jax.nn.softmax(top_v, axis=-1)
    expert_ids = grp[:, None].astype(jnp.int32) * EXPERTS_PER_GROUP + top_i.astype(jnp.int32)
    y = grouped_expert_ffn(xf, expert_ids, weights, w_gate, w_up, w_down)
    return y.reshape(B, S, D)

def setup_inputs(seed: int = 0) -> dict:
    key = jax.random.key(seed)
    ks = list(jax.random.split(key, 32))
    n_even = (DEPTH + 1) // 2
    n_odd = DEPTH // 2
    f32 = jnp.float32

    def nrm(shape, scale):
        return scale * jax.random.normal(ks.pop(0), shape, f32)

    def gain(shape):
        return 1.0 + 0.02 * jax.random.normal(ks.pop(0), shape, f32)

    u = jax.random.uniform(ks.pop(0), (n_odd, C_HEADS), f32)
    dt = jnp.exp(u * (math.log(0.1) - math.log(0.001)) + math.log(0.001))
    dt_bias = dt + jnp.log(-jnp.expm1(-dt))
    a_log = jnp.log(jax.random.uniform(ks.pop(0), (n_odd, C_HEADS), f32, minval=1.0, maxval=16.0))
    return {
        'x': nrm((BATCH, SEQ, D_MODEL), 1.0),
        'even_attn_norm': gain((n_even, D_MODEL)),
        'even_w_in': nrm((n_even, D_MODEL, EVEN_IN), D_MODEL ** -0.5),
        'a_q_norm': gain((n_even, HEAD_DIM)),
        'a_k_norm': gain((n_even, HEAD_DIM)),
        'b_q_norm': gain((n_even, HEAD_DIM)),
        'b_k_norm': gain((n_even, HEAD_DIM)),
        'b_lambda_q1': nrm((n_even, B_HEADS, HEAD_DIM), 0.1),
        'b_lambda_k1': nrm((n_even, B_HEADS, HEAD_DIM), 0.1),
        'b_lambda_q2': nrm((n_even, B_HEADS, HEAD_DIM), 0.1),
        'b_lambda_k2': nrm((n_even, B_HEADS, HEAD_DIM), 0.1),
        'b_out_norm': gain((n_even, B_VDIM)),
        'even_w_out': nrm((n_even, A_WIDTH + B_WIDTH, D_MODEL), (A_WIDTH + B_WIDTH) ** -0.5),
        'odd_attn_norm': gain((n_odd, D_MODEL)),
        'odd_w_in': nrm((n_odd, D_MODEL, ODD_IN), D_MODEL ** -0.5),
        'odd_conv_w': nrm((n_odd, CONV_W, 3 * C_WIDTH), CONV_W ** -0.5),
        'odd_a_log': a_log,
        'odd_dt_bias': dt_bias,
        'odd_out_norm': gain((n_odd, C_DV)),
        'odd_w_out': nrm((n_odd, C_WIDTH, D_MODEL), C_WIDTH ** -0.5),
        'ffn_norm': gain((DEPTH, D_MODEL)),
        'router_group_w': nrm((DEPTH, D_MODEL, N_GROUPS), D_MODEL ** -0.5),
        'router_group_b': nrm((DEPTH, N_GROUPS), 0.01),
        'router_expert_w': nrm((DEPTH, N_GROUPS, D_MODEL, EXPERTS_PER_GROUP), D_MODEL ** -0.5),
        'router_expert_b': nrm((DEPTH, N_GROUPS, EXPERTS_PER_GROUP), 0.01),
        'expert_w_gate': nrm((DEPTH, N_EXPERTS, D_MODEL, EXPERT_FF), D_MODEL ** -0.5),
        'expert_w_up': nrm((DEPTH, N_EXPERTS, D_MODEL, EXPERT_FF), D_MODEL ** -0.5),
        'expert_w_down': nrm((DEPTH, N_EXPERTS, EXPERT_FF, D_MODEL), EXPERT_FF ** -0.5),
    }

def reference(x, even_attn_norm, even_w_in, a_q_norm, a_k_norm, b_q_norm, b_k_norm,
              b_lambda_q1, b_lambda_k1, b_lambda_q2, b_lambda_k2, b_out_norm, even_w_out,
              odd_attn_norm, odd_w_in, odd_conv_w, odd_a_log, odd_dt_bias, odd_out_norm, odd_w_out,
              ffn_norm, router_group_w, router_group_b, router_expert_w, router_expert_b,
              expert_w_gate, expert_w_up, expert_w_down):
    S = x.shape[1]
    cos, sin = rope_tables(S, HEAD_DIM)
    for layer in range(DEPTH):
        i = layer // 2
        if layer % 2 == 0:
            lam_init = 0.8 - 0.6 * math.exp(-0.3 * layer)
            h = rms_norm(x, even_attn_norm[i])
            x = x + even_mixer(h, even_w_in[i], a_q_norm[i], a_k_norm[i], b_q_norm[i], b_k_norm[i],
                               b_lambda_q1[i], b_lambda_k1[i], b_lambda_q2[i], b_lambda_k2[i],
                               b_out_norm[i], even_w_out[i], lam_init, cos, sin)
        else:
            h = rms_norm(x, odd_attn_norm[i])
            x = x + odd_mixer(h, odd_w_in[i], odd_conv_w[i], odd_a_log[i], odd_dt_bias[i],
                              odd_out_norm[i], odd_w_out[i])
        h = rms_norm(x, ffn_norm[layer])
        x = x + hier_moe(h, router_group_w[layer], router_group_b[layer], router_expert_w[layer],
                         router_expert_b[layer], expert_w_gate[layer], expert_w_up[layer],
                         expert_w_down[layer])
    return x


_drawn_inputs = setup_inputs


def setup_inputs(seed=0):
    import zlib

    import numpy as np

    out = dict(_drawn_inputs(seed))
    spreads = {}
    factors = {'a_q_norm': 3.457,
     'a_k_norm': 3.96,
     'odd_out_norm': 8.754,
     'b_q_norm': 2.98,
     'router_group_b': 2.89,
     'router_expert_b': 3.077}
    for name, (base, spread) in spreads.items():
        noise = np.random.default_rng([zlib.crc32(name.encode()), seed]).standard_normal(out[name].shape)
        drawn = base * np.exp(spread * noise) if base else spread * noise
        out[name] = jnp.asarray(drawn.astype(out[name].dtype))
    for name, factor in factors.items():
        out[name] = (out[name] * factor).astype(out[name].dtype)
    return out
```

```python
from collections import namedtuple
from contextlib import ExitStack

import numpy as np
import concourse.bass as bass
from concourse import mybir

ALU = mybir.AluOpType
ACT = mybir.ActivationFunctionType
F32 = mybir.dt.float32
U32 = mybir.dt.uint32
I32 = mybir.dt.int32
AX = mybir.AxisListType

P = 128
S = 512
D = 1024
T = S // P
KC = D // P
N = 512
HEAD = 64
A_HEADS = 8
B_HEADS = 4
C_HEADS = 8
NG, EPG = 4, 8
NE = NG * EPG
FF = D // 2
EPS = 1e-6
NEG = -1e30
LAM_INIT = 0.2
CONV = 4
RING = 6
FAR = 4096
DEPTH = 2
STAGES = ('even', 'moe0', 'odd', 'moe1')
LEVELS = 7
SLOT_BLOCKS = S // P


class Order:

    def __init__(self, eng, sem):
        self.eng, self.sem, self.n = eng, sem, 0

    def __call__(self, ins):
        self.n = self.n + 1
        ins.then_inc(self.sem, 1)
        self.eng.wait_ge(self.sem, self.n)


def constants():
    pos = np.arange(S, dtype=np.float32)[:, None]
    inv = (1.0 / (np.float32(10000.0) ** (np.arange(0, HEAD, 2, dtype=np.float32) / np.float32(HEAD)))).astype(np.float32)
    ang = (pos * inv[None, :]).astype(np.float32)
    cos, sin = np.cos(ang).astype(np.float32), np.sin(ang).astype(np.float32)
    i, j = np.arange(P)[:, None], np.arange(P)[None, :]
    dil = np.full((P, T * P), NEG, np.float32)
    cau = np.full((P, T * P), NEG, np.float32)
    for d in range(T):
        dist = d * P + i - j
        count = (dist <= 128).astype(int) + (dist % 4 == 0) + (dist % 16 == 0)
        ok = (dist >= 0) & (count > 0)
        blk = slice((T - 1 - d) * P, (T - d) * P)
        dil[:, blk] = np.where(ok, np.log(np.maximum(count, 1)), NEG)
        cau[:, blk] = np.where(dist >= 0, 0.0, NEG)
    level = np.zeros((P, LEVELS, P), np.float32)
    for s in range(LEVELS):
        bi, bj = i >> s, j >> s
        level[:, s] = (bi % 2 == 1) & (bj == bi - 1)
    tok = np.arange(S).reshape(T, P).T
    return {
        "c_ident": np.eye(P, dtype=np.float32),
        "c_cos": np.concatenate([cos, cos], 1).reshape(T, P, HEAD).transpose(1, 0, 2),
        "c_sin": np.concatenate([-sin, sin], 1).reshape(T, P, HEAD).transpose(1, 0, 2),
        "c_dilated": dil,
        "c_causal": cau,
        "c_level": level,
        "c_upto": (i <= j).astype(np.float32),
        "c_before": (i < j).astype(np.float32),
        "c_decay": np.where(i <= j, 0.0, NEG).astype(np.float32),
        "c_iota": np.broadcast_to(np.arange(P, dtype=np.float32), (P, P)),
        "c_value": np.stack([2 * tok + 1, 2 * tok + 2, tok], 1).astype(np.float32),
        "c_far": (FAR + np.arange(P, dtype=np.float32))[:, None],
    }


def build(nc, io, out, stages):
    with ExitStack() as ctx:
        def sb(name, shape, dt=F32):
            return ctx.enter_context(nc.sbuf_tensor(name, shape, dt))

        def sems(stage, names):
            return namedtuple(stage, names)(*(ctx.enter_context(nc.semaphore(f"{stage}_{n}")) for n in names.split()))

        h_dram = [nc.dram_tensor(f"h_rows{i}", (S, D), F32, kind="Internal").ap() for i in range(DEPTH)]
        y_dram = [nc.dram_tensor(f"y_rows{i}", (2 * S, D), F32, kind="Internal").ap() for i in range(DEPTH)]
        x_dram = nc.dram_tensor("x_mid", (S, D), F32, kind="Internal").ap()

        ps = ctx.enter_context(nc.psum_tensor("ps", [P, 8, N], F32))
        ring = sb("ring", [P, RING, KC * N])
        buf0 = sb("buf0", [P, T * D])
        buf1 = sb("buf1", [P, T * D])
        ident = sb("ident", [P, P])
        iota = sb("iota", [P, P])
        ones = sb("ones", [P, P])
        gcols = sb("gcols", [P, 4, KC])
        small = sb("small", [P, 1000])
        count_i = sb("count_i", [P, DEPTH, NE + 1], I32)
        ARENA = 18700
        arena = sb("arena", [P, ARENA])

        small_used = [0]

        def tiny(n):
            small_used[0] += n
            assert small_used[0] <= 1000
            return small[:, small_used[0] - n:small_used[0]]

        def carve(at, n, *dims):
            assert at + n <= ARENA, (at, n)
            a = arena[:, at:at + n]
            if len(dims) == 2:
                a = a.rearrange("p (a b) -> p a b", a=dims[0])
            if len(dims) == 3:
                a = a.rearrange("p (a b c) -> p a b c", a=dims[0], b=dims[1])
            return a

        def as_tiles(b):
            return b[:, :].rearrange("p (t d) -> p t d", t=T)

        def as_cols(b):
            return b[:, :].rearrange("p (c s) -> p c s", c=KC)

        def bank(b, a=4):
            return ps[:, b, :].rearrange("p (a s) -> p a s", a=a)

        def over(col, n):
            return col.unsqueeze(2).to_broadcast([P, col.shape[1], n])

        def under(row, n):
            return row.unsqueeze(1).to_broadcast([P, n, row.shape[1]])

        al = sems("all", "const x_loaded x_tiles chunk_used stored passed")
        landed = [ctx.enter_context(nc.semaphore(f"landed{i}")) for i in range(RING)]
        in_act, in_dve = (ctx.enter_context(nc.semaphore(n)) for n in ("act_in_order", "dve_in_order"))
        nm = sems("norm", "squares meansq root rows turned cols")

        n_chunks = {"even": 8, "moe0": 3 * NE, "odd": 10, "moe1": 3 * NE}
        n_tiles = {"even": 2 * T, "moe0": T, "odd": 2 * T, "moe1": T}
        first, x_need, place = {}, {}, {}
        k = tiles = 0
        xb, hb = buf0, buf1
        for s in stages:
            first[s], x_need[s], place[s] = k, tiles, (xb, hb)
            k += n_chunks[s]
            tiles += n_tiles[s]
            if s == "odd":
                xb, hb = hb, xb
        x_last = xb
        order_of = {s: i for i, s in enumerate(stages)}
        moe_turn = {s: i for i, s in enumerate([s for s in stages if s[:3] == "moe"])}
        gain_no = {"even": 0, "moe0": 1, "odd": 2, "moe1": 3}

        def slot(k):
            return k % RING

        def chunk(k, rows=KC):
            return ring[:, slot(k), :].rearrange("p (c n) -> p c n", c=rows)

        def wait_chunk(eng, k, i=0):
            eng.wait_ge(landed[slot(k)], i * 16 + (k // RING + 1) * 16)

        xn = carve(0, T * D, T, D)
        sumsq, meansq, rootsq, rstd = tiny(T), tiny(T), tiny(T), tiny(T)

        r = sems("route", "gates exp_in logits exp_out counted placed slots tables_psum tables h_stored")
        m = sems("moe", "index x_turned x_cols silu hidden h_turned h_cols down y_left y_right back0 back1")
        gathered = [ctx.enter_context(nc.semaphore(f"gathered{i}")) for i in range(2)]
        scattered = [ctx.enter_context(nc.semaphore(f"scattered{i}")) for i in range(2)]
        ov = [sems(f"over{i}", "load gather pe act dve scatter") for i in range(DEPTH)]
        o = T * D
        wr = carve(o, KC * 36, KC, 36); o += KC * 36
        rbias = carve(o, 36); o += 36
        lg = carve(o, T * 36, T, 36); o += T * 36
        rt = carve(o, 12 * T * NE, 12, T * NE); o += 12 * T * NE
        slot_hot = carve(o, 2 * T * P, 2 * T, P); o += 2 * T * P
        values = carve(o, 2 * T * 2 * NE, 2 * T, 2 * NE); o += 2 * T * 2 * NE
        before = carve(o, P); o += P
        value = carve(o, 3 * T, 3, T); o += 3 * T
        far = carve(o, 1); o += 1
        tab = carve(o, SLOT_BLOCKS * 2 * NE, SLOT_BLOCKS, 2 * NE); o += SLOT_BLOCKS * 2 * NE
        tab_u = carve(o, SLOT_BLOCKS * 2 * NE).bitcast(U32).rearrange("p (b q e) -> p b q e", b=SLOT_BLOCKS, q=2)
        o += SLOT_BLOCKS * 2 * NE
        now_g = carve(o, 2).bitcast(U32); o += 2
        now_s = carve(o, 2).bitcast(U32); o += 2
        w_mix = carve(o, 2 * T, 2, T); o += 2 * T
        sg = carve(o, 2 * FF, 2, FF); o += 2 * FF
        hid = carve(o, 2 * FF, 2, FF); o += 2 * FF
        hidT = carve(o, 2 * FF, 2, FF); o += 2 * FF
        yb = carve(o, 2 * D, 2, D); o += 2 * D
        xg = carve(0, 2 * D, 2, D)
        xgT = carve(2 * D, 2 * D, 2, D)
        yc = carve(0, 2 * 2 * D, 2, 2 * D)
        gmax, m1, m2, least, gsum, gw, p1, p2 = (tiny(T) for _ in range(8))
        PER = NE // 2

        e = sems("even", "tables lam_exp lam proj taken squared sums mean root rotated turned qk_cols "
                 "scores masked negmax probs p_turned p_cols pv normed head_mean head_root o_turned o_cols mixed")
        qkT = carve(0, 16 * S, 16, S)
        av = carve(16 * S, T * N, T, N)
        bv = carve(20 * S, T * N, T, N)
        cos2 = carve(20 * S, T * HEAD, T, HEAD)
        sin2 = carve(20 * S + 256, T * HEAD, T, HEAD)
        qk_gain = carve(20 * S + 512, 4 * HEAD, 4, HEAD)
        lam_in = carve(20 * S + 768, 4 * B_HEADS * HEAD, 4, B_HEADS * HEAD)
        o = 24 * S
        sq, qn, t1, t2 = (carve(o + i * N, N) for i in range(4))
        rot = carve(o + 4 * N, 2 * N, 2, N)
        sm, pr, pT = (carve(o + i * 2 * N, 2 * N, 2, N) for i in range(3))
        o += 6 * N
        cg = carve(o, 4 * T * HEAD, 4, T * HEAD); o += 4 * T * HEAD
        sgn = carve(o, 4 * T * HEAD, 4, T * HEAD); o += 4 * T * HEAD
        dilated = carve(o, N); o += N
        causal = carve(o, N); o += N
        out_gain = tiny(P)
        oT = carve(0, T * D, KC, S)
        ms8, mean8, root8, rstd8 = tiny(8), tiny(8), tiny(8), tiny(8)
        row_max, neg_max, den, rden = tiny(64), tiny(64), tiny(64), tiny(64)
        lam4 = tiny(5 * B_HEADS)
        nlam = tiny(1)
        head16 = tiny(4 * 16)
        o1 = carve(24 * S + 6 * N, P)

        d = sems("odd", "consts gates_psum gates_in gates_ln g_ready sums_psum cums gates_exp proj conv taps silu "
                 "posted tok sums root unit back cols rows_in rows_psum rows_sum decay grams "
                 "xy p_psum p_sb xp x_spilled")
        d2 = sems("odd2", "ks r qs tr vn av kv st o hmean hroot z z_silu on o_turned o_cols x_back mixed")
        H4 = 4
        qTh, kTh, ktok, vtok, Yt, At = (carve(i * T * N, T * N, T, N) for i in range(6))
        o = 6 * T * N
        LT, Xm, Pm = (carve(o + i * 2 * N, 2 * N, 2, N) for i in range(3))
        cv, ks, sqq = LT, Xm, Pm
        Rr, vn, vd, qs = LT[:, 0, :], LT[:, 1, :], Xm[:, 0, :], Xm[:, 1, :]
        o += 6 * N
        St = carve(o, N, H4, P); o += N
        level = carve(o, LEVELS * P, LEVELS, P); o += LEVELS * P
        upto = carve(o, P); o += P
        decay0 = carve(o, P); o += P
        cw = carve(o, 96); o += 96
        cw_rows = carve(o, P); o += P
        w_tail = carve(o, KC * 16, KC, 16); o += KC * 16
        gn = carve(o, P); o += P
        dt_b, a_log = carve(o, C_HEADS), carve(o + C_HEADS, C_HEADS); o += 2 * C_HEADS
        (ga, gb, gabs, gexp, gbe, gln, gg, beta, Gs, nG, Gl, dG, eG, neG, eGl, eD) = (
            carve(o + i * 32, 32, T, C_HEADS) for i in range(16))
        o += 16 * 32
        ealog = carve(o, C_HEADS); o += C_HEADS
        ssq, sroot, srec, hm, hmean, hroot, hrec = (carve(o + i * 32, 32) for i in range(7))
        o += 7 * 32

        block = ctx.enter_context(nc.Block())

        UNITS = [(blk, pair, a, half) for blk in "AB" for pair in range(4) for a in range(T) for half in range(2)]
        PROJ = [(k, t) for k in range(6) for t in range(T)]
        QK_NO = {0: 0, 1: 1, 3: 2, 4: 3}
        CONSTS = 16 * 8

        def bank_done(eng, sem, n, per, k, t):
            if t < per:
                eng.wait_ge(sem, per * n + t + 1)
            else:
                eng.wait_ge(al.chunk_used, k + 1)

        PU = [(g, j, h) for g in range(2) for j in range(3) for h in range(H4)]

        def xy_no(g, tp, s, w):
            return ((g * 2 + tp) * (LEVELS + 1) + s) * 2 + w + 1

        def lv_no(g, tp, s, w):
            return ((g * 2 + tp) * LEVELS + s) * 2 + w + 1

        def odd_sp(sp, load_chunk, load_columns):
            f = first["odd"]
            w_in = io["odd_w_in"][0]
            if order_of["odd"]:
                sp.wait_ge(al.x_tiles, x_need["odd"])
            else:
                sp.wait_ge(al.x_loaded, 16 * T)
            for dst, src in ((level, io["c_level"]), (upto, io["c_upto"]), (decay0, io["c_decay"]),
                             (cw_rows[0:96, :], io["odd_conv_w"][0].rearrange("w (b p) -> (w b) p", p=P)),
                             (w_tail, w_in[:, 4 * D:4 * D + 16].rearrange("(p c) n -> p c n", c=KC)),
                             (gn, io["odd_out_norm"][0].partition_broadcast(P)),
                             (dt_b, io["odd_dt_bias"][0].partition_broadcast(P)),
                             (a_log, io["odd_a_log"][0].partition_broadcast(P))):
                sp.dma_start(dst, src).then_inc(d.consts, 16)
            for t in range(T):
                sp.dma_start(x_dram[t * P:(t + 1) * P, :], as_tiles(place["odd"][0])[:, t, :]).then_inc(d.x_spilled, 16)
            for g in range(2):
                for j in range(4):
                    load_columns(f + 4 * g + j, w_in, j * D + g * N)
            for n in range(2):
                k = f + 8 + n
                load_chunk(k, chunk(k), io["odd_w_out"][0][:, n * N:(n + 1) * N].rearrange("(c p) n -> p c n", p=P))
            sp.wait_ge(al.chunk_used, f + 8)
            sp.wait_ge(d.x_spilled, 16 * T)
            for t in range(T):
                sp.dma_start(as_tiles(place["odd"][1])[:, t, :], x_dram[t * P:(t + 1) * P, :]).then_inc(d2.x_back, 16)

        def odd_pe(pe):
            ht, f = as_cols(place["odd"][1]), first["odd"]
            oTh = as_cols(place["odd"][0])
            pe.wait_ge(d.consts, 16 * 8)
            for t in range(T):
                for c in range(KC):
                    nc.tensor.matmul(ps[:, 6, t * 16:(t + 1) * 16], ht[:, c, t * P:(t + 1) * P], w_tail[:, c, :],
                                     start=(c == 0), stop=(c == KC - 1))
            nc.tensor.transpose(ps[:, 7, 0:96], cw_rows[0:96, :], ident[0:96, 0:96]).then_inc(d.gates_psum, 1)
            pe.wait_ge(d.g_ready, 1)
            nc.tensor.matmul(ps[:, 6, 0:32], upto, gg.rearrange("p t h -> p (t h)"), start=True, stop=True)
            nc.tensor.matmul(ps[:, 6, 32:64], ones[:, :], gg.rearrange("p t h -> p (t h)"), start=True,
                             stop=True).then_inc(d.sums_psum, 1)

            def project(u):
                g, j, h = PU[u]
                k = f + 4 * g + j
                if h == 0:
                    wait_chunk(pe, k)
                if u >= 3:
                    pe.wait_ge(d.taps, u - 2)
                for c in range(KC):
                    last = nc.tensor.matmul(ps[:, u % 3, :], chunk(k)[:, c, h * P:(h + 1) * P], ht[:, c, :],
                                            start=(c == 0), stop=(c == KC - 1))
                last.then_inc(al.chunk_used if h == H4 - 1 else d.proj, 1)

            def post(u):
                g, j, h = PU[u]
                pe.wait_ge(d.silu, u + 1)
                if j == 0:
                    for t in range(T):
                        last = nc.tensor.matmul(ps[:, 5, 4 * t + h:4 * t + h + 1], sqq[:, u % 2, t * P:(t + 1) * P],
                                                ones[:, 0:1], start=True, stop=True)
                else:
                    w = 8 * g + 4 * (j - 1) + h
                    if w >= 2:
                        pe.wait_ge(d.tok, w - 1)
                    for t in range(T):
                        last = nc.tensor.transpose(ps[:, 3 + w % 2, t * P:(t + 1) * P], ks[:, u % 2, t * P:(t + 1) * P],
                                                   ident[:, :])
                last.then_inc(d.posted, 1)

            for g in range(2):
                if g:
                    pe.wait_ge(d2.o_cols, T * g)
                for u in range(12 * g, 12 * g + 12):
                    project(u)
                    if u > 12 * g:
                        post(u - 1)
                post(12 * g + 11)
                for h in range(H4):
                    pe.wait_ge(d.unit, g + 1)
                    if 4 * g + h >= 2:
                        pe.wait_ge(d.cols, 4 * g + h - 1)
                    for t in range(T):
                        last = nc.tensor.transpose(ps[:, 6 + h % 2, t * P:(t + 1) * P], ktok[:, t, h * P:(h + 1) * P],
                                                   ident[:, :])
                    last.then_inc(d.back, 1)
                for tp in range(2):
                    for w in range(2):
                        t = 2 * tp + w
                        c = T * g + t
                        pe.wait_ge(d.rows_in, c + 1)
                        nc.tensor.matmul(ps[:, w, :], ones[:, :], Pm[:, w, :], start=True, stop=True).then_inc(d.rows_psum, 1)
                        pe.wait_ge(d.cols, 4 * (g + 1))
                        for q, rhs in ((2, kTh), (4, qTh)):
                            for h in range(H4):
                                last = nc.tensor.matmul(ps[:, q + w, h * P:(h + 1) * P], kTh[:, h, t * P:(t + 1) * P],
                                                        rhs[:, h, t * P:(t + 1) * P], start=True, stop=True)
                        last.then_inc(d.grams, 1)
                    for s in range(LEVELS):
                        for w in range(2):
                            pe.wait_ge(d.xy, xy_no(g, tp, s, w))
                            for h in range(H4):
                                c = slice(h * P, (h + 1) * P)
                                last = nc.tensor.matmul(ps[:, w, c], LT[:, w, c], Xm[:, w, c], start=True, stop=True)
                            last.then_inc(d.p_psum, 1)
                        for w in range(2):
                            pe.wait_ge(d.p_sb, lv_no(g, tp, s, w))
                            for h in range(H4):
                                c = slice(h * P, (h + 1) * P)
                                if s < LEVELS - 1:
                                    nc.tensor.matmul(ps[:, 2 + w, c], Yt[:, 2 * tp + w, c], Pm[:, w, c], start=True, stop=True)
                                last = nc.tensor.matmul(ps[:, 4 + w, c], Pm[:, w, c], Yt[:, 2 * tp + w, c], start=True, stop=True)
                            last.then_inc(d.xp, 1)
                pe.wait_ge(d.xy, xy_no(g, 1, LEVELS, 1))
                for t in range(T):
                    c, tc = T * g + t, slice(t * P, (t + 1) * P)

                    def heads(b, lhs, rhs):
                        for h in range(H4):
                            last = nc.tensor.matmul(ps[:, b, h * P:(h + 1) * P], lhs(h), rhs[:, h * P:(h + 1) * P],
                                                    start=True, stop=True)
                        return last

                    if t:
                        state = St.rearrange("p h d -> p (h d)")
                        pe.wait_ge(d2.st, 3 * g + t)
                        if 3 * g + t > 1:
                            pe.wait_ge(d2.qs, 3 * g + t - 1)
                        heads(0, lambda h: kTh[:, h, tc], state)
                        heads(1, lambda h: qTh[:, h, tc], state).then_inc(d2.ks, 1)
                        pe.wait_ge(d2.r, 3 * g + t)
                    heads(2, lambda h: Yt[:, t, h * P:(h + 1) * P], Rr if t else vtok[:, t, :]).then_inc(d2.tr, 1)
                    pe.wait_ge(d2.vn, c + 1)
                    if t < T - 1:
                        heads(4, lambda h: ktok[:, t, h * P:(h + 1) * P], vd).then_inc(d2.kv, 1)
                    heads(3, lambda h: At[:, t, h * P:(h + 1) * P], vn).then_inc(d2.av, 1)
                    k = f + 4 * g + 3
                    if t == 0:
                        wait_chunk(pe, k)
                    if c >= 2:
                        pe.wait_ge(d2.z_silu, c - 1)
                    for q in range(KC):
                        last = nc.tensor.matmul(ps[:, 6 + t % 2, :], ht[:, q, tc], chunk(k)[:, q, :],
                                                start=(q == 0), stop=(q == KC - 1))
                    last.then_inc(al.chunk_used if t == T - 1 else d2.z, 1)
                for t in range(T):
                    pe.wait_ge(d2.on, T * g + t + 1)
                    if t >= 2:
                        pe.wait_ge(d2.o_cols, T * g + t - 1)
                    for h in range(H4):
                        last = nc.tensor.transpose(ps[:, t % 2, h * P:(h + 1) * P], vtok[:, t, h * P:(h + 1) * P], ident[:, :])
                    last.then_inc(d2.o_turned, 1)
            pe.wait_ge(d2.o_cols, 2 * T)
            for n in range(2):
                for t in range(T):
                    u = T * n + t
                    if t == 0:
                        wait_chunk(pe, f + 8 + n)
                    if u >= 4:
                        pe.wait_ge(al.x_tiles, x_need["odd"] + u - 3)
                    for c in range(KC):
                        last = nc.tensor.matmul(ps[:, 4 + u % 4, :], oTh[:, c, t * P:(t + 1) * P], chunk(f + 8 + n)[:, c, :],
                                                start=(c == 0), stop=(c == KC - 1))
                    last.then_inc(al.chunk_used if t == T - 1 else d2.mixed, 1)

        def odd_act(act, step):
            f = first["odd"]
            A = nc.scalar
            act.wait_ge(d.gates_in, 1)
            step(A.activation(gabs, ga, ACT.Abs))
            step(A.activation(gexp, gabs, ACT.Exp, scale=-1.0))
            A.activation(gbe, gb, ACT.Exp, scale=-1.0)
            A.activation(ealog, a_log, ACT.Exp)
            A.activation(gln, gexp, ACT.Ln, bias=1.0).then_inc(d.gates_ln, 1)
            act.wait_ge(d.cums, 1)
            A.activation(eG, Gs, ACT.Exp)
            A.activation(eGl, Gl, ACT.Exp)
            A.activation(eD, dG, ACT.Exp).then_inc(d.gates_exp, 1)

            def conv(u):
                g, j, h = PU[u]
                bank_done(act, d.proj, 3 * g + j, 3, f + 4 * g + j, h)
                if u >= 2:
                    act.wait_ge(d.silu, u - 1)
                A.activation(cv[:, u % 2, :], ps[:, u % 3, :], ACT.Copy,
                             scale=cw[:, 72 + 8 * j + 4 * g + h:73 + 8 * j + 4 * g + h]).then_inc(d.conv, 1)

            def silu(u):
                g, j, h = PU[u]
                act.wait_ge(d.taps, u + 1)
                if u >= 2:
                    act.wait_ge(d.posted, u - 1)
                if j == 0:
                    step(A.activation(qTh[:, h, :], cv[:, u % 2, :], ACT.Silu))
                    A.activation(sqq[:, u % 2, :], qTh[:, h, :], ACT.Square).then_inc(d.silu, 1)
                else:
                    A.activation(ks[:, u % 2, :], cv[:, u % 2, :], ACT.Silu).then_inc(d.silu, 1)

            for g in range(2):
                for u in range(12 * g, 12 * g + 12):
                    conv(u)
                    if u > 12 * g:
                        silu(u - 1)
                silu(12 * g + 11)
                act.wait_ge(d.sums, g + 1)
                A.activation(sroot, ssq, ACT.Sqrt).then_inc(d.root, 1)
                for c in range(T * g, T * g + T):
                    t = c % T
                    act.wait_ge(d.rows_sum, c + 1)
                    for h in range(H4):
                        last = A.activation(Yt[:, t, h * P:(h + 1) * P], Pm[:, t % 2, h * P:(h + 1) * P], ACT.Exp,
                                            bias=nG[:, t, 4 * g + h:4 * g + h + 1])
                    last.then_inc(d.decay, 1)
                for t in range(T):
                    c = T * g + t
                    if t:
                        act.wait_ge(d2.ks, 3 * g + t)
                        act.wait_ge(d2.o, c)
                        for h in range(H4):
                            last = A.activation(qs[:, h * P:(h + 1) * P], ps[:, 1, h * P:(h + 1) * P], ACT.Copy,
                                                scale=eG[:, t, 4 * g + h:4 * g + h + 1])
                        last.then_inc(d2.qs, 1)
                    bank_done(act, d2.z, g, 3, f + 4 * g + 3, t)
                    A.activation(At[:, t, :], ps[:, 6 + t % 2, :], ACT.Silu).then_inc(d2.z_silu, 1)
                act.wait_ge(d2.hmean, g + 1)
                A.activation(hroot[:, 0:16], hmean[:, 0:16], ACT.Sqrt).then_inc(d2.hroot, 1)
                if g == 0:
                    act.wait_ge(d.x_spilled, 16 * T)
                for t in range(T):
                    act.wait_ge(d2.o_turned, T * g + t + 1)
                    A.copy(as_cols(place["odd"][0])[:, 4 * g:4 * g + 4, t * P:(t + 1) * P], bank(t % 2)).then_inc(d2.o_cols, 1)

        def odd_dve(dve, step, add_mixed):
            f = first["odd"]
            V = nc.vector
            dve.wait_ge(d.gates_psum, 1)
            step(V.tensor_copy(cw, ps[:, 7, 0:96]))
            ab = ps[:, 6, 0:64].rearrange("p (t n) -> p t n", n=16)
            V.tensor_tensor(ga, ab[:, :, 0:8], under(dt_b, T), ALU.add)
            V.tensor_copy(gb, ab[:, :, 8:16]).then_inc(d.gates_in, 1)
            dve.wait_ge(d.gates_ln, 1)
            step(V.scalar_tensor_tensor(out=gln, in0=ga, scalar=0.0, in1=gln, op0=ALU.max, op1=ALU.add))
            step(V.tensor_scalar(gbe, gbe, 1.0, None, ALU.add))
            step(V.reciprocal(beta, gbe))
            V.scalar_tensor_tensor(out=gg, in0=gln, scalar=-1.0, in1=under(ealog, T), op0=ALU.mult,
                                   op1=ALU.mult).then_inc(d.g_ready, 1)
            dve.wait_ge(d.sums_psum, 1)
            tot = ps[:, 6, 0:64].rearrange("p (a t h) -> p a t h", a=2, t=T)
            V.tensor_copy(Gs, tot[:, 0])
            step(V.tensor_copy(Gl, tot[:, 1]))
            V.tensor_scalar(nG, Gs, -1.0, None, ALU.mult)
            V.tensor_tensor(dG, Gl, Gs, ALU.subtract).then_inc(d.cums, 1)
            dve.wait_ge(d.gates_exp, 1)
            step(V.tensor_scalar(neG, eG, -1.0, None, ALU.mult))

            def taps(u):
                g, j, h = PU[u]
                dve.wait_ge(d.conv, u + 1)
                for s in range(1, CONV):
                    w = cw[:, 24 * (CONV - 1 - s) + 8 * j + 4 * g + h:24 * (CONV - 1 - s) + 8 * j + 4 * g + h + 1]
                    last = V.scalar_tensor_tensor(out=cv[:, u % 2, s:], in0=ps[:, u % 3, 0:N - s], scalar=w,
                                                  in1=cv[:, u % 2, s:], op0=ALU.mult, op1=ALU.add)
                    if s < CONV - 1:
                        step(last)
                last.then_inc(d.taps, 1)

            def tokens(u):
                g, j, h = PU[u]
                dve.wait_ge(d.posted, u + 1)
                if j:
                    w = 8 * g + 4 * (j - 1) + h
                    V.tensor_copy((ktok if j == 1 else vtok)[:, :, h * P:(h + 1) * P], bank(3 + w % 2)).then_inc(d.tok, 1)
                    dve.wait_ge(d.tok, w + 1)

            for g in range(2):
                for u in range(12 * g, 12 * g + 12):
                    taps(u)
                    if u > 12 * g:
                        tokens(u - 1)
                tokens(12 * g + 11)
                step(V.tensor_scalar(ssq[:, 0:16], ps[:, 5, 0:16], EPS, None, ALU.add))
                for t in range(T):
                    step(V.tensor_tensor(St.rearrange("p h d -> p (h d)"), ktok[:, t, :], ktok[:, t, :], ALU.mult))
                    step(V.tensor_reduce(srec[:, 4 * t:4 * t + 4], St, AX.X, ALU.add))
                V.tensor_scalar(ssq[:, 16:32], srec[:, 0:16], EPS, None, ALU.add).then_inc(d.sums, 1)
                dve.wait_ge(d.root, g + 1)
                step(V.reciprocal(srec, sroot))
                step(V.tensor_scalar(srec[:, 0:16], srec[:, 0:16], float(P) ** -0.5, None, ALU.mult))
                for t in range(T):
                    rows = ktok[:, t, :].rearrange("p (h d) -> p h d", h=H4)
                    last = V.tensor_tensor(rows, rows, over(srec[:, 16 + 4 * t:20 + 4 * t], P), ALU.mult)
                last.then_inc(d.unit, 1)
                for h in range(H4):
                    dve.wait_ge(d.back, H4 * g + h + 1)
                    V.tensor_copy(kTh[:, h, :], ps[:, 6 + h % 2, :]).then_inc(d.cols, 1)
                for tp in range(2):
                    for w in range(2):
                        t = 2 * tp + w
                        V.tensor_tensor(Pm[:, w, :].rearrange("p (h i) -> p h i", h=H4), under(upto, H4),
                                        over(gg[:, t, 4 * g:4 * g + 4], P), ALU.mult).then_inc(d.rows_in, 1)
                    for w in range(2):
                        c = T * g + 2 * tp + w
                        dve.wait_ge(d.rows_psum, c + 1)
                        V.tensor_tensor(Pm[:, w, :].rearrange("p (h i) -> p h i", h=H4), bank(w), under(decay0, H4),
                                        ALU.add).then_inc(d.rows_sum, 1)
                    for w in range(2):
                        t = 2 * tp + w
                        c = T * g + t
                        dve.wait_ge(d.decay, c + 1)
                        dve.wait_ge(d.grams, c + 1)
                        for h in range(H4):
                            V.scalar_tensor_tensor(out=LT[:, w, h * P:(h + 1) * P], in0=ps[:, 2 + w, h * P:(h + 1) * P],
                                                   scalar=beta[:, t, 4 * g + h:4 * g + h + 1], in1=Yt[:, t, h * P:(h + 1) * P],
                                                   op0=ALU.mult, op1=ALU.mult)
                        step(V.tensor_tensor(At[:, t, :], ps[:, 4 + w, :], Yt[:, t, :], ALU.mult))
                        V.tensor_copy(Xm[:, w, :].rearrange("p (h i) -> p h i", h=H4), under(ident[:, :], H4))
                        V.tensor_copy(Yt[:, t, :].rearrange("p (h i) -> p h i", h=H4), under(ident[:, :], H4)).then_inc(d.xy, 1)
                    for s in range(LEVELS):
                        for w in range(2):
                            dve.wait_ge(d.p_psum, lv_no(g, tp, s, w))
                            V.tensor_tensor(Pm[:, w, :].rearrange("p (h i) -> p h i", h=H4), bank(w),
                                            under(level[:, s, :], H4), ALU.mult).then_inc(d.p_sb, 1)
                        for w in range(2):
                            dve.wait_ge(d.xp, lv_no(g, tp, s, w))
                            dve.wait_ge(d.xy, xy_no(g, tp, s, w))
                            if s < LEVELS - 1:
                                V.tensor_tensor(Xm[:, w, :], Xm[:, w, :], ps[:, 2 + w, :], ALU.subtract)
                            y = Yt[:, 2 * tp + w, :]
                            V.tensor_tensor(y, y, ps[:, 4 + w, :], ALU.subtract).then_inc(d.xy, 1)
                for t in range(T):
                    c = T * g + t
                    cols = slice(4 * g, 4 * g + 4)
                    hd = "p (h e) -> p h e"
                    if t:
                        dve.wait_ge(d2.ks, 3 * g + t)
                        for h in range(H4):
                            last = V.scalar_tensor_tensor(out=Rr[:, h * P:(h + 1) * P], in0=ps[:, 0, h * P:(h + 1) * P],
                                                          scalar=neG[:, t, 4 * g + h:4 * g + h + 1],
                                                          in1=vtok[:, t, h * P:(h + 1) * P], op0=ALU.mult, op1=ALU.add)
                        last.then_inc(d2.r, 1)
                    dve.wait_ge(d2.tr, c + 1)
                    step(V.tensor_tensor(vn.rearrange(hd, h=H4), bank(2), over(beta[:, t, cols], P), ALU.mult))
                    V.tensor_tensor(vd.rearrange(hd, h=H4), vn.rearrange(hd, h=H4), over(eD[:, t, cols], P),
                                    ALU.mult).then_inc(d2.vn, 1)
                    if t < T - 1:
                        dve.wait_ge(d2.kv, 3 * g + t + 1)
                        if t == 0:
                            V.tensor_copy(St.rearrange("p h d -> p (h d)"), ps[:, 4, :]).then_inc(d2.st, 1)
                        else:
                            for h in range(H4):
                                last = V.scalar_tensor_tensor(out=St[:, h, :], in0=St[:, h, :],
                                                              scalar=eGl[:, t, 4 * g + h:4 * g + h + 1],
                                                              in1=ps[:, 4, h * P:(h + 1) * P], op0=ALU.mult, op1=ALU.add)
                            last.then_inc(d2.st, 1)
                        dve.wait_ge(d2.st, 3 * g + t + 1)
                    dve.wait_ge(d2.av, c + 1)
                    rows = vtok[:, t, :].rearrange(hd, h=H4)
                    if t:
                        dve.wait_ge(d2.qs, 3 * g + t)
                        step(V.tensor_tensor(rows, bank(3), qs.rearrange(hd, h=H4), ALU.add))
                        V.tensor_tensor(rows, rows, over(srec[:, 4 * t:4 * t + 4], P), ALU.mult).then_inc(d2.o, 1)
                    else:
                        V.tensor_tensor(rows, bank(3), over(srec[:, 0:4], P), ALU.mult).then_inc(d2.o, 1)
                    dve.wait_ge(d2.o, c + 1)
                for t in range(T):
                    step(V.tensor_tensor(Rr, vtok[:, t, :], vtok[:, t, :], ALU.mult))
                    step(V.tensor_reduce(hm[:, 4 * t:4 * t + 4], Rr.rearrange("p (h e) -> p h e", h=H4), AX.X, ALU.add))
                V.tensor_scalar(hmean[:, 0:16], hm[:, 0:16], 1.0 / P, EPS, ALU.mult, ALU.add).then_inc(d2.hmean, 1)
                dve.wait_ge(d2.hroot, g + 1)
                step(V.reciprocal(hrec[:, 0:16], hroot[:, 0:16]))
                for t in range(T):
                    rows = vtok[:, t, :].rearrange("p (h e) -> p h e", h=H4)
                    step(V.tensor_tensor(rows, rows, over(hrec[:, 4 * t:4 * t + 4], P), ALU.mult))
                    step(V.tensor_tensor(rows, rows, under(gn, H4), ALU.mult))
                    dve.wait_ge(d2.z_silu, T * g + t + 1)
                    V.tensor_tensor(vtok[:, t, :], vtok[:, t, :], At[:, t, :], ALU.mult).then_inc(d2.on, 1)
            dve.wait_ge(d2.x_back, 16 * T)
            add_mixed(place["odd"][1], d2.mixed, "odd", 8)

        @block.sync
        def _(sp):
            def load_chunk(k, dst, src):
                if k >= RING:
                    sp.wait_ge(al.chunk_used, k - RING + 1)
                sp.dma_start(dst, src).then_inc(landed[slot(k)], 16)

            def load_columns(k, w, col):
                load_chunk(k, chunk(k), w[:, col:col + N].rearrange("(p c) n -> p c n", c=KC))

            def even():
                f = first["even"]
                for b in range(6):
                    load_columns(f + b, io["even_w_in"][0], b * N)
                for n in range(2):
                    load_columns(f + 6 + n, io["even_w_out"][0], n * N)

            def expert_load(s, i, j, e):
                L = int(s[3])
                for n, name in enumerate(("expert_w_gate", "expert_w_up", "expert_w_down")):
                    k = first[s] + 3 * j + n
                    if not isinstance(i, int) or i * RING + k >= RING:
                        sp.wait_ge(al.chunk_used, i * RING + (k - RING + 1))
                    src = io[name][L, e].rearrange("(p c) f -> p (c f)", p=P)
                    sp.dma_start(ring[:, slot(k), :], src).then_inc(landed[slot(k)], 16)

            def moe(s):
                L, v = int(s[3]), moe_turn[s]
                if order_of[s]:
                    sp.wait_ge(al.x_tiles, x_need[s])
                sp.dma_start(wr[:, :, 0:NG], io["router_group_w"][L].rearrange("(p c) g -> p c g", c=KC)).then_inc(r.gates, 16)
                for q in range(NG):
                    sp.dma_start(wr[:, :, NG + q * EPG:NG + (q + 1) * EPG],
                                 io["router_expert_w"][L, q].rearrange("(p c) e -> p c e", c=KC)).then_inc(r.gates, 16)
                sp.dma_start(rbias[:, 0:NG], io["router_group_b"][L].partition_broadcast(P)).then_inc(r.gates, 16)
                sp.dma_start(rbias[:, NG:NG + NE],
                             io["router_expert_b"][L].rearrange("g e -> (g e)").partition_broadcast(P)).then_inc(r.gates, 16)
                sp.dma_start(before, io["c_before"]).then_inc(r.gates, 16)
                sp.dma_start(value, io["c_value"]).then_inc(r.gates, 16)
                sp.dma_start(far, io["c_far"]).then_inc(r.gates, 16)
                for t in range(T):
                    sp.wait_ge(nm.rows, order_of[s] * T + t + 1)
                    sp.dma_start(h_dram[L][t * P:(t + 1) * P, :], xn[:, t, :]).then_inc(r.h_stored, 16)
                for j in range(2):
                    expert_load(s, 0, j, j)
                with sp.Fori(1, PER) as i:
                    for j in range(2):
                        expert_load(s, i, j, i * 2 + j)
                overflow(s)

            def overflow(s):
                L = int(s[3])
                f = ov[L]
                sp.wait_ge(r.tables, moe_turn[s] + 1)
                most = sp.value_load(count_i[0:1, int(s[3]), NE:NE + 1], min_val=0, max_val=S)
                with sp.If(most > P):
                    sp.wait_ge(al.chunk_used, first[s] + 3 * NE)
                    for b in range(1, SLOT_BLOCKS):
                        with sp.If(most > b * P), sp.Fori(0, NE) as q:
                            n = q + (b - 1) * NE
                            for c, name in enumerate(("expert_w_gate", "expert_w_up", "expert_w_down")):
                                sp.dma_start(ring[:, c, :], io[name][L, q].rearrange("(p c) f -> p (c f)", p=P)
                                             ).then_inc(f.load, 16)
                            sp.wait_ge(f.scatter, n * 16 + 16)
                            sp.sem_inc(f.load, 1)

            def combine(s):
                v, L = moe_turn[s], int(s[3])
                for b in range(2):
                    sp.wait_ge(scattered[b], 16 * PER * (v + 1))
                src = y_dram[L].rearrange("(t p k) d -> t p (k d)", t=T, k=2)
                for t in range(T):
                    if t >= 2:
                        sp.wait_ge(al.x_tiles, x_need[s] + t - 1)
                    sp.dma_start(yc[:, t % 2, :], src[t]).then_inc(m.back1 if t % 2 else m.back0, 16)

            for t in range(T):
                sp.dma_start(as_tiles(buf0)[:, t, :], io["x"][0, t * P:(t + 1) * P, :]).then_inc(al.x_loaded, 16)
            sp.dma_start(ident[:, :], io["c_ident"]).then_inc(al.const, 16)
            sp.dma_start(iota[:, :], io["c_iota"]).then_inc(al.const, 16)
            for q, a in enumerate((io["even_attn_norm"][0], io["ffn_norm"][0], io["odd_attn_norm"][0], io["ffn_norm"][1])):
                sp.dma_start(gcols[:, q, :], a.rearrange("(p c) -> p c", c=KC)).then_inc(al.const, 16)
            sp.dma_start(out_gain, io["b_out_norm"][0].partition_broadcast(P)).then_inc(al.const, 16)
            for s in stages:
                if s == "even":
                    for q, n in enumerate(("a_q_norm", "a_k_norm", "b_q_norm", "b_k_norm")):
                        sp.dma_start(qk_gain[:, q, :], io[n][0].partition_broadcast(P)).then_inc(e.tables, 16)
                    for q, n in enumerate(("b_lambda_q1", "b_lambda_k1", "b_lambda_q2", "b_lambda_k2")):
                        sp.dma_start(lam_in[:, q, :], io[n][0].rearrange("h d -> (h d)").partition_broadcast(P)
                                     ).then_inc(e.tables, 16)
                    for dst, n in ((cos2, "c_cos"), (sin2, "c_sin"), (dilated, "c_dilated"), (causal, "c_causal")):
                        sp.dma_start(dst, io[n]).then_inc(e.tables, 16)
                    even()
                elif s == "odd":
                    odd_sp(sp, load_chunk, load_columns)
                else:
                    moe(s)
                    combine(s)
            for t in range(T):
                sp.wait_ge(al.x_tiles, tiles - n_tiles[stages[-1]] + (t + 1 if stages[-1][:3] == "moe" else T + t + 1))
                sp.dma_start(out[0, t * P:(t + 1) * P, :], as_tiles(x_last)[:, t, :]).then_inc(al.stored, 16)
            sp.wait_ge(al.stored, 16 * T)

        @block.scalar
        def _(act):
            step = Order(act, in_act)

            def norm(s):
                x, o = as_tiles(place[s][0]), order_of[s]
                if o:
                    act.wait_ge(al.x_tiles, x_need[s])
                for t in range(T):
                    if o == 0:
                        act.wait_ge(al.x_loaded, 16 * T)
                    nc.scalar.activation(xn[:, t, :], x[:, t, :], ACT.Square,
                                         accum_out=sumsq[:, t:t + 1]).then_inc(nm.squares, 1)
                act.wait_ge(nm.meansq, o + 1)
                nc.scalar.activation(rootsq, meansq, ACT.Sqrt).then_inc(nm.root, 1)

            def even():
                f = first["even"]
                act.wait_ge(e.lam_exp, 1)
                nc.scalar.activation(lam4[:, 8:16], lam4[:, 0:8], ACT.Exp).then_inc(e.lam, 1)
                for k, t in PROJ:
                    if k not in QK_NO:
                        continue
                    w = QK_NO[k] * T + t
                    u = T * k + t
                    bank_done(act, e.proj, k, 3, f + k, t)
                    if w:
                        act.wait_ge(e.sums, w)
                    nc.scalar.activation(sq, ps[:, u % 4, :], ACT.Square).then_inc(e.squared, 1)
                    act.wait_ge(e.mean, w + 1)
                    nc.scalar.activation(root8, mean8, ACT.Sqrt).then_inc(e.root, 1)
                for i, (blk, pair, a, half) in enumerate(UNITS):
                    nk = (a + 1) * P
                    act.wait_ge(e.negmax, i + 1)
                    if i >= 2:
                        act.wait_ge(e.p_turned, i - 1)
                    nc.scalar.activation(pr[:, i % 2, 0:nk], sm[:, i % 2, 0:nk], ACT.Exp, bias=neg_max[:, i:i + 1],
                                         accum_out=den[:, i:i + 1]).then_inc(e.probs, 1)
                act.wait_ge(e.head_mean, 1)
                nc.scalar.activation(head16[:, 32:48], head16[:, 16:32], ACT.Sqrt).then_inc(e.head_root, 1)
                for i in range(2 * T):
                    act.wait_ge(e.o_turned, i + 1)
                    t, q = i // 2, i % 2
                    nc.scalar.copy(oT[:, 4 * q:4 * q + 4, t * P:(t + 1) * P], bank(i % 4)).then_inc(e.o_cols, 1)

            def expert(s, i, b):
                n = 2 * i + (b + NE * moe_turn[s])
                k = first[s] + 3 * b
                act.wait_ge(al.chunk_used, i * RING + k + 1)
                nc.scalar.activation(sg[:, b, :], ps[:, 2, :], ACT.Silu).then_inc(m.silu, 1)
                act.wait_ge(m.h_turned, n + 1)
                nc.scalar.copy(hidT[:, b, :], ps[:, 4, :]).then_inc(m.h_cols, 1)
                act.wait_ge(m.down, n + 1)
                if not isinstance(i, int) or i + moe_turn[s] > 0:
                    act.wait_ge(scattered[b], i * 16 + 16 * PER * moe_turn[s])
                nc.scalar.copy(yb[:, b, 0:N], ps[:, 5, :]).then_inc(m.y_left, 1)

            def moe(s):
                v = moe_turn[s]
                act.wait_ge(r.exp_in, 2 * v + 1)
                nc.scalar.activation(rt[:, 11, 0:T * NG], rt[:, 10, 0:T * NG], ACT.Exp).then_inc(r.exp_out, 1)
                act.wait_ge(r.exp_in, 2 * v + 2)
                nc.scalar.activation(w_mix[:, 1, :], w_mix[:, 0, :], ACT.Exp).then_inc(r.exp_out, 1)
                for b in range(2):
                    expert(s, 0, b)
                with act.Fori(1, PER) as i:
                    for b in range(2):
                        expert(s, i, b)
                over(s)

            def over(s):
                f = ov[int(s[3])]
                most = act.value_load(count_i[0:1, int(s[3]), NE:NE + 1], min_val=0, max_val=S)
                with act.If(most > P):
                    for b in range(1, SLOT_BLOCKS):
                        with act.If(most > b * P), act.Fori(0, NE) as q:
                            n = q + (b - 1) * NE
                            act.wait_ge(f.pe, n * 4 + 2)
                            nc.scalar.activation(sg[:, 0, :], ps[:, 2, :], ACT.Silu).then_inc(f.act, 1)

            for s in stages:
                norm(s)
                if s == "even":
                    even()
                elif s == "odd":
                    odd_act(act, step)
                else:
                    moe(s)

        @block.tensor
        def _(pe):
            def turn(dst, rows, q):
                v = rows.rearrange("p (m c) -> p c m", c=KC)
                for j in range(4):
                    last = nc.tensor.transpose(ps[:, dst, j * P:(j + 1) * P], v[:, 4 * q + j, :], ident[:, :])
                return last

            def norm(s):
                o = order_of[s]
                if o == 0:
                    pe.wait_ge(al.const, CONSTS)
                for i in range(2 * T):
                    pe.wait_ge(nm.rows, o * T + i // 2 + 1)
                    if i >= 4:
                        pe.wait_ge(nm.cols, o * 2 * T + i - 3)
                    turn(i % 4, xn[:, i // 2, :], i % 2).then_inc(nm.turned, 1)
                pe.wait_ge(nm.cols, (o + 1) * 2 * T)

            def even():
                ht, f = as_cols(place["even"][1]), first["even"]

                def project(k, t):
                    u = T * k + t
                    if t == 0:
                        wait_chunk(pe, f + k)
                    if u >= 4:
                        pe.wait_ge(e.taken, u - 3)
                    for c in range(KC):
                        last = nc.tensor.matmul(ps[:, u % 4, :], ht[:, c, t * P:(t + 1) * P], chunk(f + k)[:, c, :],
                                                start=(c == 0), stop=(c == KC - 1))
                    last.then_inc(al.chunk_used if t == T - 1 else e.proj, 1)

                def turn_qk(w):
                    pe.wait_ge(e.rotated, w + 1)
                    if w >= 2:
                        pe.wait_ge(e.qk_cols, w - 1)
                    for j in range(4):
                        last = nc.tensor.transpose(ps[:, 4 + w % 2, j * P:(j + 1) * P],
                                                   rot[:, w % 2, j * P:(j + 1) * P], ident[:, :])
                    last.then_inc(e.turned, 1)

                behind = None
                for k, t in PROJ:
                    project(k, t)
                    if behind is not None:
                        turn_qk(behind)
                    behind = QK_NO[k] * T + t if k in QK_NO else None
                pe.wait_ge(e.qk_cols, 16)
                pe.wait_ge(e.taken, 24)

                def scores(i):
                    blk, pair, a, half = UNITS[i]
                    q0 = 0 if blk == "A" else 8
                    rows = slice(half * HEAD, half * HEAD + HEAD)
                    if i >= 2:
                        pe.wait_ge(e.masked, i - 1)
                    nc.tensor.matmul(ps[:, i % 2, 0:(a + 1) * P], qkT[rows, q0 + pair, a * P:(a + 1) * P],
                                     qkT[rows, q0 + 4 + pair, 0:(a + 1) * P], start=True, stop=True).then_inc(e.scores, 1)

                def turn_probs(i):
                    a = UNITS[i][2]
                    pe.wait_ge(e.probs, i + 1)
                    if i >= 2:
                        pe.wait_ge(e.p_cols, i - 1)
                    for j in range(a + 1):
                        last = nc.tensor.transpose(ps[:, 2 + i % 2, j * P:(j + 1) * P],
                                                   pr[:, i % 2, j * P:(j + 1) * P], ident[:, :])
                    last.then_inc(e.p_turned, 1)

                def weigh(i):
                    blk, pair, a, half = UNITS[i]
                    pe.wait_ge(e.p_cols, i + 1)
                    if i >= 2:
                        pe.wait_ge(e.normed, i - 1)
                    for j in range(a + 1):
                        if blk == "A":
                            v = av[:, j, (2 * pair + half) * HEAD:(2 * pair + half + 1) * HEAD]
                        else:
                            v = bv[:, j, pair * P:(pair + 1) * P]
                        last = nc.tensor.matmul(ps[:, 4 + i % 2, 0:v.shape[1]], pT[:, i % 2, j * P:(j + 1) * P], v,
                                                start=(j == 0), stop=(j == a))
                    last.then_inc(e.pv, 1)

                for i in range(len(UNITS) + 2):
                    if i < len(UNITS):
                        scores(i)
                    if 1 <= i <= len(UNITS):
                        turn_probs(i - 1)
                    if i >= 2:
                        weigh(i - 2)

                attn = as_tiles(place["even"][1])
                for i in range(2 * T):
                    pe.wait_ge(e.normed, len(UNITS) + i // 2 + 1)
                    if i >= 4:
                        pe.wait_ge(e.o_cols, i - 3)
                    turn(i % 4, attn[:, i // 2, :], i % 2).then_inc(e.o_turned, 1)
                pe.wait_ge(e.o_cols, 2 * T)
                for n in range(2):
                    for t in range(T):
                        u = T * n + t
                        if t == 0:
                            wait_chunk(pe, f + 6 + n)
                        if u >= 4:
                            pe.wait_ge(al.x_tiles, x_need["even"] + u - 3)
                        for c in range(KC):
                            last = nc.tensor.matmul(ps[:, 4 + u % 4, :], oT[:, c, t * P:(t + 1) * P],
                                                    chunk(f + 6 + n)[:, c, :], start=(c == 0), stop=(c == KC - 1))
                        last.then_inc(al.chunk_used if t == T - 1 else e.mixed, 1)

            def turn_x(s, i, b):
                v = moe_turn[s]
                n = 2 * i + (b + NE * v)
                pe.wait_ge(gathered[b], i * 16 + 16 * (1 + PER * v))
                for q in range(2):
                    if not isinstance(n, int) or n:
                        pe.wait_ge(m.x_cols, 2 * n + (q - 1))
                    turn(q, xg[:, b, :], q).then_inc(m.x_turned, 1)

            def expert(s, i, b, last_one=False):
                v, k = moe_turn[s], first[s] + 3 * b
                n = 2 * i + (b + NE * v)
                pe.wait_ge(m.x_cols, 2 * n + 2)
                for q in range(2):
                    wait_chunk(pe, k + q, i)
                    if not isinstance(n, int) or n:
                        pe.wait_ge(m.hidden if q else m.silu, n)
                    for c in range(KC):
                        last = nc.tensor.matmul(ps[:, 2 + q, :], xgT[:, b, c * P:(c + 1) * P], chunk(k + q)[:, c, :],
                                                start=(c == 0), stop=(c == KC - 1))
                    last.then_inc(al.chunk_used, 1)
                if not last_one:
                    turn_x(s, i + b, 1 - b)
                pe.wait_ge(m.hidden, n + 1)
                if not isinstance(n, int) or n:
                    pe.wait_ge(m.h_cols, n)
                rows = hid[:, b, :].rearrange("p (m c) -> p c m", c=4)
                for j in range(4):
                    last = nc.tensor.transpose(ps[:, 4, j * P:(j + 1) * P], rows[:, j, :], ident[:, :])
                last.then_inc(m.h_turned, 1)
                wait_chunk(pe, k + 2, i)
                pe.wait_ge(m.h_cols, n + 1)
                for q in range(2):
                    if not isinstance(n, int) or n:
                        pe.wait_ge(m.y_right if q else m.y_left, n)
                    for c in range(FF // P):
                        last = nc.tensor.matmul(ps[:, 5 + q, :], hidT[:, b, c * P:(c + 1) * P],
                                                chunk(k + 2, FF // P)[:, c, q * N:(q + 1) * N],
                                                start=(c == 0), stop=(c == FF // P - 1))
                    last.then_inc(al.chunk_used if q else m.down, 1)

            def moe(s):
                v = moe_turn[s]
                ht = as_cols(place[s][1])
                pe.wait_ge(r.gates, 16 * 10 * (v + 1))
                for t in range(T):
                    for c in range(KC):
                        last = nc.tensor.matmul(ps[:, 4, t * 36:(t + 1) * 36], ht[:, c, t * P:(t + 1) * P],
                                                wr[:, c, :], start=(c == 0), stop=(c == KC - 1))
                last.then_inc(r.logits, 1)
                pe.wait_ge(r.counted, v + 1)
                chosen = rt[:, 9, :].rearrange("p (t e) -> p t e", t=T)
                for t in range(T):
                    for q in range(t + 1):
                        nc.tensor.matmul(ps[:, 5, t * NE:(t + 1) * NE], before if q == t else ones[:, :],
                                         chosen[:, q, :], start=(q == 0), stop=(q == t))
                for q in range(T):
                    last = nc.tensor.matmul(ps[:, 6, 0:NE], ones[:, :], chosen[:, q, :], start=(q == 0), stop=(q == T - 1))
                last.then_inc(r.placed, 1)
                for b in range(SLOT_BLOCKS):
                    pe.wait_ge(r.slots, SLOT_BLOCKS * v + b + 1)
                    for i in range(2 * T):
                        last = nc.tensor.matmul(ps[:, 7, b * 2 * NE:(b + 1) * 2 * NE], slot_hot[:, i, :], values[:, i, :],
                                                start=(i == 0), stop=(i == 2 * T - 1))
                    last.then_inc(r.tables_psum, 1)
                turn_x(s, 0, 0)
                for b in range(2):
                    expert(s, 0, b)
                with pe.Fori(1, PER - 1) as i:
                    for b in range(2):
                        expert(s, i, b)
                for b in range(2):
                    expert(s, PER - 1, b, last_one=(b == 1))
                over(s)

            def over(s):
                f = ov[int(s[3])]
                most = pe.value_load(count_i[0:1, int(s[3]), NE:NE + 1], min_val=0, max_val=S)
                with pe.If(most > P):
                    for b in range(1, SLOT_BLOCKS):
                        with pe.If(most > b * P), pe.Fori(0, NE) as q:
                            n = q + (b - 1) * NE
                            pe.wait_ge(f.gather, n * 16 + 16)
                            for h in range(2):
                                last = turn(h, xg[:, 0, :], h)
                            last.then_inc(f.pe, 1)
                            pe.wait_ge(f.dve, n * 6 + 2)
                            pe.wait_ge(f.load, n * 49 + 48)
                            for h in range(2):
                                for c in range(KC):
                                    last = nc.tensor.matmul(ps[:, 2 + h, :], xgT[:, 0, c * P:(c + 1) * P],
                                                            ring[:, h, c * N:(c + 1) * N],
                                                            start=(c == 0), stop=(c == KC - 1))
                            last.then_inc(f.pe, 1)
                            pe.wait_ge(f.dve, n * 6 + 3)
                            rows = hid[:, 0, :].rearrange("p (m c) -> p c m", c=4)
                            for j in range(4):
                                last = nc.tensor.transpose(ps[:, 4, j * P:(j + 1) * P], rows[:, j, :], ident[:, :])
                            last.then_inc(f.pe, 1)
                            pe.wait_ge(f.dve, n * 6 + 4)
                            for h in range(2):
                                for c in range(FF // P):
                                    last = nc.tensor.matmul(ps[:, 5 + h, :], hidT[:, 0, c * P:(c + 1) * P],
                                                            ring[:, 2, c * D + h * N:c * D + (h + 1) * N],
                                                            start=(c == 0), stop=(c == FF // P - 1))
                            last.then_inc(f.pe, 1)

            for s in stages:
                norm(s)
                if s == "even":
                    even()
                elif s == "odd":
                    odd_pe(pe)
                else:
                    moe(s)

        @block.vector
        def _(dve):
            step = Order(dve, in_dve)
            V = nc.vector

            def norm(s):
                x, ht, o = as_tiles(place[s][0]), as_cols(place[s][1]), order_of[s]
                dve.wait_ge(nm.squares, (o + 1) * T)
                V.tensor_scalar(meansq, sumsq, 1.0 / D, EPS, ALU.mult, ALU.add).then_inc(nm.meansq, 1)
                dve.wait_ge(nm.root, o + 1)
                step(V.reciprocal(rstd, rootsq))
                for t in range(T):
                    V.tensor_scalar(xn[:, t, :], x[:, t, :], rstd[:, t:t + 1], None, ALU.mult).then_inc(nm.rows, 1)
                if o == 0:
                    dve.wait_ge(al.const, CONSTS)
                for i in range(2 * T):
                    t, q = i // 2, i % 2
                    dve.wait_ge(nm.turned, o * 2 * T + i + 1)
                    gain = gcols[:, gain_no[s], 4 * q:4 * q + 4]
                    V.tensor_tensor(ht[:, 4 * q:4 * q + 4, t * P:(t + 1) * P], bank(i % 4), over(gain, P),
                                    ALU.mult).then_inc(nm.cols, 1)

            def even_tables():
                dve.wait_ge(e.tables, 16 * 12)
                for q in range(4):
                    by = 0.125 if q % 2 == 0 else 1.0
                    c = cg[:, q, :].rearrange("p (t h) -> p t h", t=T)
                    n = sgn[:, q, :].rearrange("p (t h) -> p t h", t=T)
                    V.scalar_tensor_tensor(out=c, in0=cos2, scalar=by, in1=under(qk_gain[:, q, :], T),
                                           op0=ALU.mult, op1=ALU.mult)
                    V.scalar_tensor_tensor(out=n[:, :, 0:32], in0=sin2[:, :, 0:32], scalar=by,
                                           in1=under(qk_gain[:, q, 32:64], T), op0=ALU.mult, op1=ALU.mult)
                    step(V.scalar_tensor_tensor(out=n[:, :, 32:64], in0=sin2[:, :, 32:64], scalar=by,
                                                in1=under(qk_gain[:, q, 0:32], T), op0=ALU.mult, op1=ALU.mult))
                for q in range(2):
                    step(V.tensor_tensor(t1[:, 0:256], lam_in[:, 2 * q, :], lam_in[:, 2 * q + 1, :], ALU.mult))
                    last = V.tensor_reduce(lam4[:, 4 * q:4 * q + 4], t1[:, 0:256].rearrange("p (h d) -> p h d", h=4),
                                           AX.X, ALU.add)
                    if q == 0:
                        step(last)
                last.then_inc(e.lam_exp, 1)
                dve.wait_ge(e.lam, 1)
                step(V.tensor_tensor(lam4[:, 16:20], lam4[:, 12:16], lam4[:, 8:12], ALU.subtract))
                step(V.tensor_scalar(lam4[:, 16:20], lam4[:, 16:20], -LAM_INIT, None, ALU.add))
                step(V.tensor_scalar(out_gain, out_gain, 1.0 - LAM_INIT, None, ALU.mult))

            def even():
                f = first["even"]
                even_tables()

                def qk_unit(k, t):
                    q, u = QK_NO[k], T * k + t
                    w = q * T + t
                    x = ps[:, u % 4, :].rearrange("p (h d) -> p h d", d=HEAD)
                    dve.wait_ge(e.squared, w + 1)
                    V.tensor_reduce(ms8, sq.rearrange("p (h d) -> p h d", d=HEAD), AX.X, ALU.add).then_inc(e.sums, 1)
                    dve.wait_ge(e.sums, w + 1)
                    V.tensor_scalar(mean8, ms8, 1.0 / HEAD, EPS, ALU.mult, ALU.add).then_inc(e.mean, 1)
                    dve.wait_ge(e.root, w + 1)
                    step(V.reciprocal(rstd8, root8))
                    qv, av_, bv_, rv = (z.rearrange("p (h d) -> p h d", d=HEAD) for z in (qn, t1, t2, rot[:, w % 2, :]))
                    V.tensor_tensor(qv, x, over(rstd8, HEAD), ALU.mult).then_inc(e.taken, 1)
                    dve.wait_ge(e.taken, u + 1)
                    c, n = cg[:, q, t * HEAD:(t + 1) * HEAD], sgn[:, q, t * HEAD:(t + 1) * HEAD]
                    V.tensor_tensor(av_, qv, under(c, 8), ALU.mult)
                    V.tensor_tensor(bv_[:, :, 0:32], qv[:, :, 32:64], under(n[:, 0:32], 8), ALU.mult)
                    step(V.tensor_tensor(bv_[:, :, 32:64], qv[:, :, 0:32], under(n[:, 32:64], 8), ALU.mult))
                    if w >= 2:
                        dve.wait_ge(e.turned, w - 1)
                    V.tensor_tensor(rot[:, w % 2, :], t1, t2, ALU.add).then_inc(e.rotated, 1)

                def qk_columns(w):
                    q, t = w // T, w % T
                    dve.wait_ge(e.turned, w + 1)
                    V.tensor_copy(qkT[:, 4 * q:4 * q + 4, t * P:(t + 1) * P], bank(4 + w % 2)).then_inc(e.qk_cols, 1)

                behind = None
                for k, t in PROJ:
                    bank_done(dve, e.proj, k, 3, f + k, t)
                    if k in QK_NO:
                        qk_unit(k, t)
                    else:
                        V.tensor_copy((av if k == 2 else bv)[:, t, :], ps[:, (T * k + t) % 4, :]).then_inc(e.taken, 1)
                    if behind is not None:
                        qk_columns(behind)
                    behind = QK_NO[k] * T + t if k in QK_NO else None

                def mask(i):
                    blk, pair, a, half = UNITS[i]
                    nk = (a + 1) * P
                    dve.wait_ge(e.scores, i + 1)
                    if i >= 2:
                        dve.wait_ge(e.probs, i - 1)
                    V.tensor_tensor_reduce(sm[:, i % 2, 0:nk], ps[:, i % 2, 0:nk],
                                           (dilated if blk == "A" else causal)[:, N - nk:N], 1.0, NEG,
                                           ALU.add, ALU.max, row_max[:, i:i + 1]).then_inc(e.masked, 1)
                    dve.wait_ge(e.masked, i + 1)
                    V.tensor_scalar(neg_max[:, i:i + 1], row_max[:, i:i + 1], -1.0, None, ALU.mult).then_inc(e.negmax, 1)

                def prob_columns(i):
                    nk = (UNITS[i][2] + 1) * P
                    dve.wait_ge(e.p_turned, i + 1)
                    if i >= 2:
                        dve.wait_ge(e.pv, i - 1)
                    V.tensor_copy(pT[:, i % 2, 0:nk], ps[:, 2 + i % 2, 0:nk]).then_inc(e.p_cols, 1)

                attn = as_tiles(place["even"][1])

                def normalise(i):
                    blk, pair, a, half = UNITS[i]
                    dve.wait_ge(e.pv, i + 1)
                    step(V.reciprocal(rden[:, i:i + 1], den[:, i:i + 1]))
                    acc, rd = ps[:, 4 + i % 2, :], rden[:, i:i + 1]
                    if blk == "A":
                        h = 2 * pair + half
                        last = V.tensor_scalar(attn[:, a, h * HEAD:(h + 1) * HEAD], acc[:, 0:HEAD], rd, None, ALU.mult)
                    elif half == 0:
                        last = V.tensor_scalar(o1, acc[:, 0:P], rd, None, ALU.mult)
                    else:
                        step(V.tensor_tensor(nlam, rd, lam4[:, 16 + pair:17 + pair], ALU.mult))
                        last = V.scalar_tensor_tensor(out=attn[:, a, N + pair * P:N + (pair + 1) * P], in0=acc[:, 0:P],
                                                      scalar=nlam, in1=o1, op0=ALU.mult, op1=ALU.add)
                    last.then_inc(e.normed, 1)
                    dve.wait_ge(e.normed, i + 1)

                for i in range(len(UNITS) + 2):
                    if i < len(UNITS):
                        mask(i)
                    if 1 <= i <= len(UNITS):
                        prob_columns(i - 1)
                    if i >= 2:
                        normalise(i - 2)

                for a in range(T):
                    step(V.tensor_tensor(t2, attn[:, a, N:D], attn[:, a, N:D], ALU.mult))
                    step(V.tensor_reduce(head16[:, 4 * a:4 * a + 4], t2.rearrange("p (h d) -> p h d", h=4), AX.X, ALU.add))
                V.tensor_scalar(head16[:, 16:32], head16[:, 0:16], 1.0 / P, EPS, ALU.mult, ALU.add).then_inc(e.head_mean, 1)
                dve.wait_ge(e.head_root, 1)
                step(V.reciprocal(head16[:, 48:64], head16[:, 32:48]))
                for a in range(T):
                    rows = attn[:, a, N:D].rearrange("p (h d) -> p h d", h=4)
                    step(V.tensor_tensor(rows, rows, over(head16[:, 48 + 4 * a:52 + 4 * a], P), ALU.mult))
                    V.tensor_tensor(rows, rows, under(out_gain, 4), ALU.mult).then_inc(e.normed, 1)
                add_mixed(place["even"][0], e.mixed, "even", 6)

            def add_mixed(xbuf, ready, s, c):
                x = as_tiles(xbuf)
                for n in range(2):
                    for t in range(T):
                        u = T * n + t
                        bank_done(dve, ready, n, 3, first[s] + c + n, t)
                        V.tensor_tensor(x[:, t, n * N:(n + 1) * N], x[:, t, n * N:(n + 1) * N], ps[:, 4 + u % 4, :],
                                        ALU.add).then_inc(al.x_tiles, 1)

            def pick(hot, scores, best):
                n = scores.shape[2]
                step(V.tensor_reduce(best, scores, AX.X, ALU.max))
                step(V.tensor_tensor(hot, scores, over(best, n), ALU.is_equal))
                step(V.scalar_tensor_tensor(out=hot, in0=hot, scalar=-1000.0, in1=under(iota[:, 0:n], T),
                                            op0=ALU.mult, op1=ALU.add))
                step(V.tensor_reduce(least, hot, AX.X, ALU.min))
                step(V.tensor_tensor(hot, hot, over(least, n), ALU.is_equal))

            def route(s):
                v = moe_turn[s]

                def grid(i, n=NE):
                    return rt[:, i, 0:T * n].rearrange("p (t e) -> p t e", t=T)

                dve.wait_ge(r.logits, v + 1)
                step(V.tensor_tensor(lg, ps[:, 4, 0:T * 36].rearrange("p (t e) -> p t e", t=T), under(rbias, T), ALU.add))
                lgg, lge = lg[:, :, 0:NG], lg[:, :, NG:NG + NE]
                group, el, hot1, hot2 = grid(0, NG), grid(1), grid(2), grid(3)
                pick(group, lgg, gmax)
                V.tensor_tensor(grid(10, NG), lgg, over(gmax, NG), ALU.subtract).then_inc(r.exp_in, 1)
                step(V.tensor_scalar(grid(4, NG), group, -1.0, -NEG, ALU.add, ALU.mult))
                for q in range(NG):
                    last = V.tensor_tensor(el[:, :, q * EPG:(q + 1) * EPG], lge[:, :, q * EPG:(q + 1) * EPG],
                                           grid(4, NG)[:, :, q:q + 1].to_broadcast([P, T, EPG]), ALU.add)
                step(last)
                pick(hot1, el, m1)
                step(V.scalar_tensor_tensor(out=el, in0=hot1, scalar=2 * NEG, in1=el, op0=ALU.mult, op1=ALU.add))
                pick(hot2, el, m2)
                V.tensor_tensor(w_mix[:, 0, :], m2, m1, ALU.subtract).then_inc(r.exp_in, 1)
                chosen = grid(9)
                V.tensor_tensor(chosen, hot1, hot2, ALU.add).then_inc(r.counted, 1)
                dve.wait_ge(r.exp_out, 2 * v + 1)
                step(V.tensor_reduce(gsum, grid(11, NG), AX.X, ALU.add))
                step(V.reciprocal(gw, gsum))
                dve.wait_ge(r.exp_out, 2 * v + 2)
                step(V.tensor_scalar(p1, w_mix[:, 1, :], 1.0, None, ALU.add))
                step(V.reciprocal(p2, p1))
                step(V.tensor_tensor(w_mix[:, 0, :], gw, p2, ALU.mult))
                step(V.tensor_tensor(w_mix[:, 1, :], w_mix[:, 0, :], w_mix[:, 1, :], ALU.mult))
                dve.wait_ge(r.placed, v + 1)
                pos = grid(5)
                step(V.tensor_copy(pos, ps[:, 5, 0:T * NE].rearrange("p (t e) -> p t e", t=T)))
                step(V.tensor_reduce(gsum[:, 0:1], ps[:, 6, 0:NE], AX.X, ALU.max))
                V.tensor_copy(count_i[:, int(s[3]), 0:NE], ps[:, 6, 0:NE])
                V.tensor_copy(count_i[:, int(s[3]), NE:NE + 1], gsum[:, 0:1])
                for j, (hot, p) in enumerate(((hot1, p1), (hot2, p2))):
                    step(V.tensor_tensor(grid(6), hot, pos, ALU.mult))
                    step(V.tensor_reduce(p, grid(6), AX.X, ALU.add))
                    vals = values[:, j * T:(j + 1) * T, :]
                    V.tensor_tensor(vals[:, :, 0:NE], hot, over(value[:, j, :], NE), ALU.mult)
                    step(V.tensor_tensor(vals[:, :, NE:2 * NE], hot, over(value[:, 2, :], NE), ALU.mult))
                for b in range(SLOT_BLOCKS):
                    if b:
                        dve.wait_ge(r.tables_psum, SLOT_BLOCKS * v + b)
                        step(V.tensor_scalar(p1, p1, -float(P), None, ALU.add))
                        step(V.tensor_scalar(p2, p2, -float(P), None, ALU.add))
                    V.tensor_tensor(slot_hot[:, 0:T, :], under(iota[:, :], T), over(p1, P), ALU.is_equal)
                    V.tensor_tensor(slot_hot[:, T:2 * T, :], under(iota[:, :], T), over(p2, P),
                                    ALU.is_equal).then_inc(r.slots, 1)
                dve.wait_ge(r.tables_psum, SLOT_BLOCKS * (v + 1))
                step(V.tensor_copy(tab.rearrange("p b e -> p (b e)"), ps[:, 7, 0:SLOT_BLOCKS * 2 * NE]))
                a, t = tab[:, :, 0:NE], tab[:, :, NE:2 * NE]
                gone = rt[:, 6, :].rearrange("p (b e) -> p b e", b=SLOT_BLOCKS)
                step(V.tensor_scalar(gone, a, 0.0, far, ALU.is_equal, ALU.mult))
                step(V.tensor_tensor(t, t, gone, ALU.add))
                step(V.scalar_tensor_tensor(out=a, in0=a, scalar=-1.0, in1=gone, op0=ALU.add, op1=ALU.add))
                V.tensor_copy(tab_u[:, :, 0, :], a)
                V.tensor_copy(tab_u[:, :, 1, :], t).then_inc(r.tables, 1)
                dve.wait_ge(r.tables, v + 1)
                dve.wait_ge(r.h_stored, 16 * T * (v + 1))

            def index(s, i, b):
                if not isinstance(i, int) or i + moe_turn[s] > 0:
                    dve.wait_ge(gathered[b], i * 16 + 16 * PER * moe_turn[s])
                V.tensor_copy(now_g[:, b:b + 1], tab_u[:, 0, 1, bass.ds(i * 2 + b, 1)]).then_inc(m.index, 1)

            def columns(s, i, b):
                n = 2 * i + (b + NE * moe_turn[s])
                for q in range(2):
                    dve.wait_ge(m.x_turned, 2 * n + (q + 1))
                    V.tensor_tensor(xgT[:, b, :].rearrange("p (c s) -> p c s", c=KC)[:, 4 * q:4 * q + 4, :], bank(q),
                                    over(gcols[:, gain_no[s], 4 * q:4 * q + 4], P), ALU.mult).then_inc(m.x_cols, 1)

            def expert(s, i, b, has_next=True, has_after=True):
                v, k = moe_turn[s], first[s] + 3 * b
                n = 2 * i + (b + NE * v)
                dve.wait_ge(m.silu, n + 1)
                dve.wait_ge(al.chunk_used, i * RING + k + 2)
                V.tensor_tensor(hid[:, b, :], sg[:, b, :], ps[:, 3, :], ALU.mult).then_inc(m.hidden, 1)
                if has_after:
                    index(s, i + 1, b)
                if has_next:
                    columns(s, i + b, 1 - b)
                if not isinstance(i, int) or i + v > 0:
                    dve.wait_ge(scattered[b], i * 16 + 16 * PER * v)
                V.tensor_copy(now_s[:, b:b + 1], tab_u[:, 0, 0, bass.ds(i * 2 + b, 1)])
                dve.wait_ge(al.chunk_used, i * RING + k + 3)
                V.tensor_copy(yb[:, b, N:D], ps[:, 6, :]).then_inc(m.y_right, 1)

            def moe(s):
                v = moe_turn[s]
                route(s)
                index(s, 0, 0)
                index(s, 0, 1)
                columns(s, 0, 0)
                for b in range(2):
                    expert(s, 0, b)
                with dve.Fori(1, PER - 1) as i:
                    for b in range(2):
                        expert(s, i, b)
                for b in range(2):
                    expert(s, PER - 1, b, has_next=(b == 0), has_after=False)
                over_blocks(s)
                x = as_tiles(place[s][0])
                for t in range(T):
                    dve.wait_ge(m.back1 if t % 2 else m.back0, 16 * (T // 2 * v + t // 2 + 1))
                    for k in range(2):
                        last = V.scalar_tensor_tensor(out=x[:, t, :], in0=yc[:, t % 2, k * D:(k + 1) * D],
                                                      scalar=w_mix[:, k, t:t + 1], in1=x[:, t, :],
                                                      op0=ALU.mult, op1=ALU.add)
                        if k == 0:
                            step(last)
                    last.then_inc(al.x_tiles, 1)

            def over_blocks(s):
                f = ov[int(s[3])]
                v = moe_turn[s]
                most = dve.value_load(count_i[0:1, int(s[3]), NE:NE + 1], min_val=0, max_val=S)
                with dve.If(most > P):
                    for b in range(2):
                        dve.wait_ge(scattered[b], 16 * PER * (v + 1))
                    for b in range(1, SLOT_BLOCKS):
                        with dve.If(most > b * P), dve.Fori(0, NE) as q:
                            n = q + (b - 1) * NE
                            V.tensor_copy(now_g[:, 0:1], tab_u[:, b, 1, bass.ds(q, 1)])
                            V.tensor_copy(now_s[:, 0:1], tab_u[:, b, 0, bass.ds(q, 1)]).then_inc(f.dve, 1)
                            dve.wait_ge(f.pe, n * 4 + 1)
                            for h in range(2):
                                last = V.tensor_tensor(xgT[:, 0, :].rearrange("p (c s) -> p c s", c=KC)[:, 4 * h:4 * h + 4, :],
                                                       bank(h), over(gcols[:, gain_no[s], 4 * h:4 * h + 4], P), ALU.mult)
                            last.then_inc(f.dve, 1)
                            dve.wait_ge(f.act, n + 1)
                            V.tensor_tensor(hid[:, 0, :], sg[:, 0, :], ps[:, 3, :], ALU.mult).then_inc(f.dve, 1)
                            dve.wait_ge(f.pe, n * 4 + 3)
                            V.tensor_copy(hidT[:, 0, :], ps[:, 4, :]).then_inc(f.dve, 1)
                            dve.wait_ge(f.pe, n * 4 + 4)
                            V.tensor_copy(yb[:, 0, 0:N], ps[:, 5, :])
                            V.tensor_copy(yb[:, 0, N:D], ps[:, 6, :]).then_inc(f.dve, 1)
                            dve.wait_ge(f.scatter, n * 16 + 16)
                            dve.sem_inc(f.dve, 1)

            for s in stages:
                norm(s)
                if s == "even":
                    even()
                elif s == "odd":
                    odd_dve(dve, step, add_mixed)
                else:
                    moe(s)

        @block.gpsimd
        def _(pool):
            pool.memset(ones[:, :], 1.0).then_inc(al.const, 16)
            last_row, last_assignment = pool.to_reg(S - 1), pool.to_reg(2 * S - 1)

            def gather(s, i, b):
                L, v = int(s[3]), moe_turn[s]
                n = 2 * i + (b + NE * v)
                pool.wait_ge(m.index, n + 1)
                if not isinstance(n, int) or n >= 2:
                    pool.wait_ge(m.x_cols, 2 * n - 2)
                pool.sem_inc(al.passed, 1)
                pool.indirect_dma_start(xg[:, b, :], None, h_dram[L], bass.IndirectOffsetOnAxis(ap=now_g[:, b:b + 1], axis=0),
                                        bounds_check=last_row, oob_is_err=False).then_inc(gathered[b], 16)

            def scatter(s, i, b):
                L, v = int(s[3]), moe_turn[s]
                n = 2 * i + (b + NE * v)
                pool.wait_ge(m.y_left, n + 1)
                pool.wait_ge(m.y_right, n + 1)
                pool.sem_inc(al.passed, 1)
                pool.indirect_dma_start(y_dram[L], bass.IndirectOffsetOnAxis(ap=now_s[:, b:b + 1], axis=0), yb[:, b, :], None,
                                        bounds_check=last_assignment, oob_is_err=False).then_inc(scattered[b], 16)

            def moe(s):
                v, L = moe_turn[s], int(s[3])
                f = ov[L]
                pool.wait_ge(r.h_stored, 16 * T * (v + 1))
                gather(s, 0, 0)
                gather(s, 0, 1)
                for b in range(2):
                    gather(s, 1, b)
                    scatter(s, 0, b)
                with pool.Fori(1, PER - 1) as i:
                    for b in range(2):
                        gather(s, i + 1, b)
                        scatter(s, i, b)
                for b in range(2):
                    scatter(s, PER - 1, b)
                most = pool.value_load(count_i[0:1, int(s[3]), NE:NE + 1], min_val=0, max_val=S)
                with pool.If(most > P):
                    for b in range(1, SLOT_BLOCKS):
                        with pool.If(most > b * P), pool.Fori(0, NE) as q:
                            n = q + (b - 1) * NE
                            pool.wait_ge(f.dve, n * 6 + 1)
                            pool.sem_inc(al.passed, 1)
                            pool.indirect_dma_start(xg[:, 0, :], None, h_dram[L],
                                                    bass.IndirectOffsetOnAxis(ap=now_g[:, 0:1], axis=0),
                                                    bounds_check=last_row, oob_is_err=False).then_inc(f.gather, 16)
                            pool.wait_ge(f.dve, n * 6 + 5)
                            pool.sem_inc(al.passed, 1)
                            pool.indirect_dma_start(y_dram[L], bass.IndirectOffsetOnAxis(ap=now_s[:, 0:1], axis=0),
                                                    yb[:, 0, :], None,
                                                    bounds_check=last_assignment, oob_is_err=False).then_inc(f.scatter, 16)
                            pool.wait_ge(f.scatter, n * 16 + 16)
                            pool.sem_inc(al.passed, 1)

            for s in stages:
                if s[:3] == "moe":
                    moe(s)

    return nc


def kernel(**inputs):
    import numpy as _np
    import concourse.bacc as _bacc
    from concourse import mybir as _mybir
    from concourse.bass_utils import run_bass_kernel_spmd as _run

    nc = _bacc.Bacc("TRN2", target_bir_lowering=False, num_devices=1)
    arrays, io = {}, {}
    for name, a in list(inputs.items()) + list(constants().items()):
        a = _np.ascontiguousarray(a)
        arrays[f"in_{name}_dram"] = a
        io[name] = nc.dram_tensor(f"in_{name}_dram", a.shape, _mybir.dt.from_np(a.dtype), kind="ExternalInput").ap()
    out = nc.dram_tensor("out_0_dram", (1, S, D), _mybir.dt.from_np(_np.dtype("float32")), kind="ExternalOutput").ap()
    build(nc, io, out, STAGES)
    r = _run(nc, [arrays], core_ids=[0])
    return r.results[0]["out_0_dram"]
```

```python
from collections import namedtuple
from contextlib import ExitStack

import numpy as np
import concourse.bass as bass
from concourse import mybir

ALU = mybir.AluOpType
ACT = mybir.ActivationFunctionType
F32 = mybir.dt.float32
U32 = mybir.dt.uint32
I32 = mybir.dt.int32
AX = mybir.AxisListType

P = 128
S = 512
D = 1024
T = S // P
KC = D // P
N = 512
HEAD = 64
A_HEADS = 8
B_HEADS = 4
C_HEADS = 8
NG, EPG = 4, 8
NE = NG * EPG
FF = D // 2
EPS = 1e-6
NEG = -1e30
LAM_INIT = 0.2
CONV = 4
RING = 6
FAR = 4096
DEPTH = 2
STAGES = ('even', 'moe0', 'odd', 'moe1')
LEVELS = 7
SLOTS = 64
SLOT_BLOCKS = S // SLOTS


class Order:

    def __init__(self, eng, sem):
        self.eng, self.sem, self.n = eng, sem, 0

    def __call__(self, ins):
        self.n = self.n + 1
        ins.then_inc(self.sem, 1)
        self.eng.wait_ge(self.sem, self.n)


def constants():
    pos = np.arange(S, dtype=np.float32)[:, None]
    inv = (1.0 / (np.float32(10000.0) ** (np.arange(0, HEAD, 2, dtype=np.float32) / np.float32(HEAD)))).astype(np.float32)
    ang = (pos * inv[None, :]).astype(np.float32)
    cos, sin = np.cos(ang).astype(np.float32), np.sin(ang).astype(np.float32)
    i, j = np.arange(P)[:, None], np.arange(P)[None, :]
    dil = np.full((P, T * P), NEG, np.float32)
    cau = np.full((P, T * P), NEG, np.float32)
    for d in range(T):
        dist = d * P + i - j
        count = (dist <= 128).astype(int) + (dist % 4 == 0) + (dist % 16 == 0)
        ok = (dist >= 0) & (count > 0)
        blk = slice((T - 1 - d) * P, (T - d) * P)
        dil[:, blk] = np.where(ok, np.log(np.maximum(count, 1)), NEG)
        cau[:, blk] = np.where(dist >= 0, 0.0, NEG)
    level = np.zeros((P, LEVELS, P), np.float32)
    for s in range(LEVELS):
        bi, bj = i >> s, j >> s
        level[:, s] = (bi % 2 == 1) & (bj == bi - 1)
    tok = np.arange(S).reshape(T, P).T
    return {
        "c_ident": np.eye(P, dtype=np.float32),
        "c_cos": np.concatenate([cos, cos], 1).reshape(T, P, HEAD).transpose(1, 0, 2),
        "c_sin": np.concatenate([-sin, sin], 1).reshape(T, P, HEAD).transpose(1, 0, 2),
        "c_dilated": dil,
        "c_causal": cau,
        "c_level": level,
        "c_upto": (i <= j).astype(np.float32),
        "c_before": (i < j).astype(np.float32),
        "c_decay": np.where(i <= j, 0.0, NEG).astype(np.float32),
        "c_iota": np.broadcast_to(np.arange(P, dtype=np.float32), (P, P)),
        "c_value": np.stack([2 * tok + 1, 2 * tok + 2, tok], 1).astype(np.float32),
        "c_far": (FAR + np.arange(P, dtype=np.float32))[:, None],
    }


def build(nc, io, out, stages):
    with ExitStack() as ctx:
        def sb(name, shape, dt=F32):
            return ctx.enter_context(nc.sbuf_tensor(name, shape, dt))

        def sems(stage, names):
            return namedtuple(stage, names)(*(ctx.enter_context(nc.semaphore(f"{stage}_{n}")) for n in names.split()))

        h_dram = [nc.dram_tensor(f"h_rows{i}", (S, D), F32, kind="Internal").ap() for i in range(DEPTH)]
        y_dram = [nc.dram_tensor(f"y_rows{i}", (2 * S, D), F32, kind="Internal").ap() for i in range(DEPTH)]
        x_dram = nc.dram_tensor("x_mid", (S, D), F32, kind="Internal").ap()

        ps = ctx.enter_context(nc.psum_tensor("ps", [P, 8, N], F32))
        ring = sb("ring", [P, RING, KC * N])
        buf0 = sb("buf0", [P, T * D])
        buf1 = sb("buf1", [P, T * D])
        ident = sb("ident", [P, P])
        iota = sb("iota", [P, P])
        ones = sb("ones", [P, P])
        gcols = sb("gcols", [P, 4, KC])
        small = sb("small", [P, 1000])
        count_i = sb("count_i", [P, DEPTH, NE + 1], I32)
        wr = sb("wr", [P, KC, 36])
        rbias = sb("rbias", [P, 36])
        before = sb("before", [P, P])
        value = sb("value", [P, 3, T])
        far = sb("far", [P, 1])
        ARENA = 18440
        arena = sb("arena", [P, ARENA])

        small_used = [0]

        def tiny(n):
            small_used[0] += n
            assert small_used[0] <= 1000
            return small[:, small_used[0] - n:small_used[0]]

        def carve(at, n, *dims):
            assert at + n <= ARENA, (at, n)
            a = arena[:, at:at + n]
            if len(dims) == 2:
                a = a.rearrange("p (a b) -> p a b", a=dims[0])
            if len(dims) == 3:
                a = a.rearrange("p (a b c) -> p a b c", a=dims[0], b=dims[1])
            return a

        def as_tiles(b):
            return b[:, :].rearrange("p (t d) -> p t d", t=T)

        def as_cols(b):
            return b[:, :].rearrange("p (c s) -> p c s", c=KC)

        def bank(b, a=4):
            return ps[:, b, :].rearrange("p (a s) -> p a s", a=a)

        def over(col, n):
            return col.unsqueeze(2).to_broadcast([P, col.shape[1], n])

        def under(row, n):
            return row.unsqueeze(1).to_broadcast([P, n, row.shape[1]])

        al = sems("all", "const x_tiles chunk_used stored passed")
        landed = [ctx.enter_context(nc.semaphore(f"landed{i}")) for i in range(RING)]
        in_act, in_dve = (ctx.enter_context(nc.semaphore(n)) for n in ("act_in_order", "dve_in_order"))
        x_landed = [ctx.enter_context(nc.semaphore(f"x_landed{t}")) for t in range(T)]
        nm = sems("norm", "squares meansq root rows turned cols")

        n_chunks = {"even": 8, "moe0": 3 * NE, "odd": 10, "moe1": 3 * NE}
        n_tiles = {"even": 2 * T, "moe0": T, "odd": 2 * T, "moe1": T}
        first, x_need, place = {}, {}, {}
        k = tiles = 0
        xb, hb = buf0, buf1
        for s in stages:
            first[s], x_need[s], place[s] = k, tiles, (xb, hb)
            k += n_chunks[s]
            tiles += n_tiles[s]
            if s == "odd":
                xb, hb = hb, xb
        x_last = xb
        order_of = {s: i for i, s in enumerate(stages)}
        moe_turn = {s: i for i, s in enumerate([s for s in stages if s[:3] == "moe"])}
        gain_no = {"even": 0, "moe0": 1, "odd": 2, "moe1": 3}

        def slot(k):
            return k % RING

        def chunk(k, rows=KC):
            return ring[:, slot(k), :].rearrange("p (c n) -> p c n", c=rows)

        def wait_chunk(eng, k, i=0):
            eng.wait_ge(landed[slot(k)], i * 16 + (k // RING + 1) * 16)

        xn = carve(0, T * D, T, D)
        sumsq, meansq, rootsq, rstd = tiny(T), tiny(T), tiny(T), tiny(T)

        r = sems("route", "gates exp_in logits exp_out counted placed slots tables_psum tables h_stored")
        m = sems("moe", "index x_turned x_cols silu hidden h_turned h_cols down y_left y_right")
        back = [ctx.enter_context(nc.semaphore(f"rows_back{t}")) for t in range(T)]
        gathered = [ctx.enter_context(nc.semaphore(f"gathered{i}")) for i in range(2)]
        scattered = [ctx.enter_context(nc.semaphore(f"scattered{i}")) for i in range(2)]
        ov = [sems(f"over{i}", "load gather pe act dve scatter hot tab order") for i in range(DEPTH)]
        o = T * D
        lg = carve(o, T * 36, T, 36); o += T * 36
        rt = carve(o, 12 * T * NE, 12, T * NE); o += 12 * T * NE
        slot_hot = carve(o, 2 * T * SLOTS, 2 * T, SLOTS); o += 2 * T * SLOTS
        values = carve(o, 2 * T * 2 * NE, 2 * T, 2 * NE); o += 2 * T * 2 * NE
        tab = carve(o, 2 * NE)[0:SLOTS]; o += 2 * NE
        tab_u = carve(o, 2 * NE)[0:SLOTS].bitcast(U32).rearrange("p (q e) -> p q e", q=2); o += 2 * NE
        now_g = carve(o, 2)[0:SLOTS].bitcast(U32); o += 2
        now_s = carve(o, 2)[0:SLOTS].bitcast(U32); o += 2
        w_mix = tiny(2 * T).rearrange("p (k t) -> p k t", k=2)
        sg = carve(o, 2 * FF, 2, FF)[SLOTS:2 * SLOTS]; o += 2 * FF
        hid = carve(o, 2 * FF, 2, FF)[0:SLOTS]; o += 2 * FF
        yb = carve(o, 2 * D, 2, D)[0:SLOTS]; o += 2 * D
        hidT = carve(o, FF // P * 2 * SLOTS, 2, FF // P * SLOTS); o += FF // P * 2 * SLOTS
        xg = carve(0, 2 * D, 2, D)[0:SLOTS]
        xgT = carve(2 * D, 2 * KC * SLOTS, 2, KC * SLOTS)
        yc = carve(T * D, T * 2 * D, T, 2 * D)
        gmax, m1, m2, least, gsum, gw, p1, p2 = (tiny(T) for _ in range(8))
        PER = NE // 2

        e = sems("even", "tables lam_exp lam proj taken squared sums mean root rotated turned qk_cols "
                 "scores masked negmax probs p_turned p_cols pv normed head_mean head_root o_turned o_cols mixed")
        qkT = carve(0, 16 * S, 16, S)
        av = carve(16 * S, T * N, T, N)
        bv = carve(20 * S, T * N, T, N)
        cos2 = carve(20 * S, T * HEAD, T, HEAD)
        sin2 = carve(20 * S + 256, T * HEAD, T, HEAD)
        qk_gain = carve(20 * S + 512, 4 * HEAD, 4, HEAD)
        lam_in = carve(20 * S + 768, 4 * B_HEADS * HEAD, 4, B_HEADS * HEAD)
        o = 24 * S
        sq, qn, t1, t2 = (carve(o + i * N, N) for i in range(4))
        rot = carve(o + 4 * N, 2 * N, 2, N)
        sm, pr, pT = (carve(o + i * 2 * N, 2 * N, 2, N) for i in range(3))
        o += 6 * N
        cg = carve(o, 4 * T * HEAD, 4, T * HEAD); o += 4 * T * HEAD
        sgn = carve(o, 4 * T * HEAD, 4, T * HEAD); o += 4 * T * HEAD
        dilated = carve(o, N); o += N
        causal = carve(o, N); o += N
        out_gain = tiny(P)
        oT = carve(T * D, T * D, KC, S)
        ms8, mean8, root8, rstd8 = tiny(8), tiny(8), tiny(8), tiny(8)
        row_max, neg_max, den, rden = tiny(64), tiny(64), tiny(64), tiny(64)
        lam4 = tiny(5 * B_HEADS)
        nlam = tiny(1)
        head16 = tiny(4 * 16)
        o1 = carve(24 * S + 6 * N, P)

        d = sems("odd", "consts gates_psum gates_in gates_ln g_ready sums_psum cums gates_exp proj conv taps silu "
                 "posted tok sums root unit back cols rows_in rows_psum rows_sum decay grams "
                 "xy p_psum p_sb xp y_psum y_sb x_spilled")
        d2 = sems("odd2", "ks r qs tr vn av kv st o hmean hroot z z_silu on o_turned o_cols x_back mixed")
        H4 = 4
        qTh, kTh, ktok, vtok, Yt, At = (carve(i * T * N, T * N, T, N) for i in range(6))
        o = 6 * T * N
        LT, Xm, Pm = (carve(o + i * 2 * N, 2 * N, 2, N) for i in range(3))
        cv, ks, sqq = LT, Xm, Pm
        Rr, vn, vd, qs = LT[:, 0, :], LT[:, 1, :], Xm[:, 0, :], Xm[:, 1, :]
        o += 6 * N
        St = carve(o, N, H4, P); o += N
        level = carve(o, LEVELS * P, LEVELS, P); o += LEVELS * P
        upto = carve(o, P); o += P
        decay0 = carve(o, P); o += P
        cw = carve(o, 96); o += 96
        cw_rows = carve(o, P); o += P
        w_tail = carve(o, KC * 16, KC, 16); o += KC * 16
        gn = carve(o, P); o += P
        dt_b, a_log = carve(o, C_HEADS), carve(o + C_HEADS, C_HEADS); o += 2 * C_HEADS
        (ga, gb, gabs, gexp, gbe, gln, gg, beta, Gs, nG, Gl, dG, eG, neG, eGl, eD) = (
            carve(o + i * 32, 32, T, C_HEADS) for i in range(16))
        o += 16 * 32
        ealog = carve(o, C_HEADS); o += C_HEADS
        ssq, sroot, srec, hm, hmean, hroot, hrec = (carve(o + i * 32, 32) for i in range(7))
        o += 7 * 32

        block = ctx.enter_context(nc.Block())

        UNITS = [(blk, pair, a, half) for blk in "AB" for pair in range(4) for a in range(T) for half in range(2)]
        PROJ = [(k, t) for k in range(6) for t in range(T)]
        QK_NO = {0: 0, 1: 1, 3: 2, 4: 3}
        CONSTS = 16 * 8

        def bank_done(eng, sem, n, per, k, t):
            if t < per:
                eng.wait_ge(sem, per * n + t + 1)
            else:
                eng.wait_ge(al.chunk_used, k + 1)

        PU = [(g, j, h) for g in range(2) for j in range(3) for h in range(H4)]

        def xy_no(g, tp, s, w):
            return ((g * 2 + tp) * (LEVELS + 1) + s) * 2 + w + 1

        def p_no(g, tp, s, w):
            return ((g * 2 + tp) * LEVELS + s) * 2 + w + 1

        def wp_no(g, tp, s, w):
            return ((g * 2 + tp) * (LEVELS - 1) + s - 1) * 2 + w + 1

        def y_no(g, tp, s, w):
            return ((g * 2 + tp) * (LEVELS - 1) + s) * 2 + w + 1

        def odd_columns(load_columns, n):
            load_columns(first["odd"] + n, io["odd_w_in"][0], (n % 4) * D + n // 4 * N)

        def odd_prefetch(load_columns, chunks):
            for n in chunks:
                odd_columns(load_columns, n)

        def odd_tables(sp):
            w_in = io["odd_w_in"][0]
            if order_of["odd"]:
                sp.wait_ge(al.x_tiles, x_need["odd"])
            else:
                for t in range(T):
                    sp.wait_ge(x_landed[t], 16)
            for dst, src in ((level, io["c_level"]), (upto, io["c_upto"]), (decay0, io["c_decay"]),
                             (cw_rows[0:96, :], io["odd_conv_w"][0].rearrange("w (b p) -> (w b) p", p=P)),
                             (w_tail, w_in[:, 4 * D:4 * D + 16].rearrange("(p c) n -> p c n", c=KC)),
                             (gn, io["odd_out_norm"][0].partition_broadcast(P)),
                             (dt_b, io["odd_dt_bias"][0].partition_broadcast(P)),
                             (a_log, io["odd_a_log"][0].partition_broadcast(P))):
                sp.dma_start(dst, src).then_inc(d.consts, 16)

        def odd_sp(sp, load_chunk, load_columns):
            f = first["odd"]
            for t in range(T):
                sp.dma_start(x_dram[t * P:(t + 1) * P, :], as_tiles(place["odd"][0])[:, t, :]).then_inc(d.x_spilled, 16)
            for n in range(RING, 8):
                odd_columns(load_columns, n)
            for n in range(2):
                k = f + 8 + n
                load_chunk(k, chunk(k), io["odd_w_out"][0][:, n * N:(n + 1) * N].rearrange("(c p) n -> p c n", p=P))
            sp.wait_ge(al.chunk_used, f + 8)
            sp.wait_ge(d.x_spilled, 16 * T)
            for t in range(T):
                sp.dma_start(as_tiles(place["odd"][1])[:, t, :], x_dram[t * P:(t + 1) * P, :]).then_inc(d2.x_back, 16)

        def odd_pe(pe):
            ht, f = as_cols(place["odd"][1]), first["odd"]
            oTh = as_cols(place["odd"][0])
            pe.wait_ge(d.consts, 16 * 8)
            for t in range(T):
                for c in range(KC):
                    nc.tensor.matmul(ps[:, 6, t * 16:(t + 1) * 16], ht[:, c, t * P:(t + 1) * P], w_tail[:, c, :],
                                     start=(c == 0), stop=(c == KC - 1))
            nc.tensor.transpose(ps[:, 7, 0:96], cw_rows[0:96, :], ident[0:96, 0:96]).then_inc(d.gates_psum, 1)

            def running_sums():
                pe.wait_ge(d.g_ready, 1)
                nc.tensor.matmul(ps[:, 6, 0:32], upto, gg.rearrange("p t h -> p (t h)"), start=True, stop=True)
                nc.tensor.matmul(ps[:, 6, 32:64], ones[:, :], gg.rearrange("p t h -> p (t h)"), start=True,
                                 stop=True).then_inc(d.sums_psum, 1)

            def project(u):
                g, j, h = PU[u]
                k = f + 4 * g + j
                if h == 0:
                    wait_chunk(pe, k)
                if u >= 3:
                    pe.wait_ge(d.taps, u - 2)
                for c in range(KC):
                    last = nc.tensor.matmul(ps[:, u % 3, :], chunk(k)[:, c, h * P:(h + 1) * P], ht[:, c, :],
                                            start=(c == 0), stop=(c == KC - 1))
                last.then_inc(al.chunk_used if h == H4 - 1 else d.proj, 1)

            def post(u):
                g, j, h = PU[u]
                pe.wait_ge(d.silu, u + 1)
                if j == 0:
                    for t in range(T):
                        last = nc.tensor.matmul(ps[:, 5, 4 * t + h:4 * t + h + 1], sqq[:, u % 2, t * P:(t + 1) * P],
                                                ones[:, 0:1], start=True, stop=True)
                else:
                    w = 8 * g + 4 * (j - 1) + h
                    if w >= 2:
                        pe.wait_ge(d.tok, w - 1)
                    for t in range(T):
                        last = nc.tensor.transpose(ps[:, 3 + w % 2, t * P:(t + 1) * P], ks[:, u % 2, t * P:(t + 1) * P],
                                                   ident[:, :])
                last.then_inc(d.posted, 1)

            def turn_keys(g, h):
                pe.wait_ge(d.unit, g + 1)
                if 4 * g + h >= 2:
                    pe.wait_ge(d.cols, 4 * g + h - 1)
                for t in range(T):
                    last = nc.tensor.transpose(ps[:, 6 + h % 2, t * P:(t + 1) * P], ktok[:, t, h * P:(h + 1) * P],
                                               ident[:, :])
                last.then_inc(d.back, 1)

            for g in range(2):
                if g:
                    pe.wait_ge(d2.o_cols, T * g)
                for u in range(12 * g, 12 * g + 12):
                    project(u)
                    if u == 0:
                        running_sums()
                    if u > 12 * g:
                        post(u - 1)
                    if u >= 12 * g + 10:
                        turn_keys(g, 2 * (u - 12 * g - 10))
                        turn_keys(g, 2 * (u - 12 * g - 10) + 1)
                post(12 * g + 11)
                for tp in range(2):
                    for w in range(2):
                        t = 2 * tp + w
                        c = T * g + t
                        pe.wait_ge(d.rows_in, c + 1)
                        nc.tensor.matmul(ps[:, w, :], ones[:, :], Pm[:, w, :], start=True, stop=True).then_inc(d.rows_psum, 1)
                        pe.wait_ge(d.cols, 4 * (g + 1))
                        for q, rhs in ((2, kTh), (4, qTh)):
                            for h in range(H4):
                                last = nc.tensor.matmul(ps[:, q + w, h * P:(h + 1) * P], kTh[:, h, t * P:(t + 1) * P],
                                                        rhs[:, h, t * P:(t + 1) * P], start=True, stop=True)
                        last.then_inc(d.grams, 1)
                    def turn_all(b, rows):
                        for h in range(H4):
                            last = nc.tensor.transpose(ps[:, b, h * P:(h + 1) * P], rows[:, h * P:(h + 1) * P], ident[:, :])
                        return last

                    def times(b, lhs, rhs):
                        for h in range(H4):
                            c = slice(h * P, (h + 1) * P)
                            last = nc.tensor.matmul(ps[:, b, c], lhs[:, c], rhs[:, c], start=True, stop=True)
                        return last

                    for w in range(2):
                        pe.wait_ge(d.xy, xy_no(g, tp, 0, w))
                        turn_all(w, LT[:, w, :]).then_inc(d.p_psum, 1)
                    for s in range(1, LEVELS):
                        for w in range(2):
                            pe.wait_ge(d.xy, xy_no(g, tp, s, w))
                            turn_all(4 + w, Xm[:, w, :]).then_inc(d.y_psum, 1)
                            times(w, LT[:, w, :], Xm[:, w, :]).then_inc(d.p_psum, 1)
                        for w in range(2):
                            y = Yt[:, 2 * tp + w, :]
                            pe.wait_ge(d.p_sb, p_no(g, tp, s, w))
                            pe.wait_ge(d.y_sb, y_no(g, tp, s - 1, w))
                            if s < LEVELS - 1:
                                times(2 + w, y, Pm[:, w, :]).then_inc(d.xp, 1)
                            else:
                                times(4 + w, Pm[:, w, :], y).then_inc(d.xp, 1)
                pe.wait_ge(d.xy, xy_no(g, 1, LEVELS, 1))
                for t in range(T):
                    c, tc = T * g + t, slice(t * P, (t + 1) * P)

                    def heads(b, lhs, rhs):
                        for h in range(H4):
                            last = nc.tensor.matmul(ps[:, b, h * P:(h + 1) * P], lhs(h), rhs[:, h * P:(h + 1) * P],
                                                    start=True, stop=True)
                        return last

                    if t:
                        state = St.rearrange("p h d -> p (h d)")
                        pe.wait_ge(d2.st, 3 * g + t)
                        if 3 * g + t > 1:
                            pe.wait_ge(d2.qs, 3 * g + t - 1)
                        heads(0, lambda h: kTh[:, h, tc], state)
                        heads(1, lambda h: qTh[:, h, tc], state).then_inc(d2.ks, 1)
                        pe.wait_ge(d2.r, 3 * g + t)
                    heads(2, lambda h: Yt[:, t, h * P:(h + 1) * P], Rr if t else vtok[:, t, :]).then_inc(d2.tr, 1)
                    pe.wait_ge(d2.vn, c + 1)
                    if t < T - 1:
                        heads(4, lambda h: ktok[:, t, h * P:(h + 1) * P], vd).then_inc(d2.kv, 1)
                    heads(3, lambda h: At[:, t, h * P:(h + 1) * P], vn).then_inc(d2.av, 1)
                    k = f + 4 * g + 3
                    if t == 0:
                        wait_chunk(pe, k)
                    if c >= 2:
                        pe.wait_ge(d2.z_silu, c - 1)
                    for q in range(KC):
                        last = nc.tensor.matmul(ps[:, 6 + t % 2, :], ht[:, q, tc], chunk(k)[:, q, :],
                                                start=(q == 0), stop=(q == KC - 1))
                    last.then_inc(al.chunk_used if t == T - 1 else d2.z, 1)
                for t in range(T):
                    pe.wait_ge(d2.on, T * g + t + 1)
                    if t >= 2:
                        pe.wait_ge(d2.o_cols, T * g + t - 1)
                    for h in range(H4):
                        last = nc.tensor.transpose(ps[:, t % 2, h * P:(h + 1) * P], vtok[:, t, h * P:(h + 1) * P], ident[:, :])
                    last.then_inc(d2.o_turned, 1)
            pe.wait_ge(d2.o_cols, 2 * T)
            for n in range(2):
                for t in range(T):
                    u = T * n + t
                    if t == 0:
                        wait_chunk(pe, f + 8 + n)
                    if u >= 4:
                        pe.wait_ge(al.x_tiles, x_need["odd"] + u - 3)
                    for c in range(KC):
                        last = nc.tensor.matmul(ps[:, 4 + u % 4, :], oTh[:, c, t * P:(t + 1) * P], chunk(f + 8 + n)[:, c, :],
                                                start=(c == 0), stop=(c == KC - 1))
                    last.then_inc(al.chunk_used if t == T - 1 else d2.mixed, 1)

        def odd_act(act, step):
            f = first["odd"]
            A = nc.scalar
            act.wait_ge(d.gates_in, 1)
            step(A.activation(gabs, ga, ACT.Abs))
            step(A.activation(gexp, gabs, ACT.Exp, scale=-1.0))
            A.activation(gbe, gb, ACT.Exp, scale=-1.0)
            A.activation(ealog, a_log, ACT.Exp)
            A.activation(gln, gexp, ACT.Ln, bias=1.0).then_inc(d.gates_ln, 1)
            act.wait_ge(d.cums, 1)
            A.activation(eG, Gs, ACT.Exp)
            A.activation(eGl, Gl, ACT.Exp)
            A.activation(eD, dG, ACT.Exp).then_inc(d.gates_exp, 1)

            def conv(u):
                g, j, h = PU[u]
                bank_done(act, d.proj, 3 * g + j, 3, f + 4 * g + j, h)
                if u >= 2:
                    act.wait_ge(d.silu, u - 1)
                A.activation(cv[:, u % 2, :], ps[:, u % 3, :], ACT.Copy,
                             scale=cw[:, 72 + 8 * j + 4 * g + h:73 + 8 * j + 4 * g + h]).then_inc(d.conv, 1)

            def silu(u):
                g, j, h = PU[u]
                act.wait_ge(d.taps, u + 1)
                if u >= 2:
                    act.wait_ge(d.posted, u - 1)
                if j == 0:
                    step(A.activation(qTh[:, h, :], cv[:, u % 2, :], ACT.Silu))
                    A.activation(sqq[:, u % 2, :], qTh[:, h, :], ACT.Square).then_inc(d.silu, 1)
                else:
                    A.activation(ks[:, u % 2, :], cv[:, u % 2, :], ACT.Silu).then_inc(d.silu, 1)

            for g in range(2):
                for u in range(12 * g, 12 * g + 12):
                    if u > 12 * g:
                        silu(u - 1)
                    conv(u)
                    if u == 12 * g + 9:
                        act.wait_ge(d.sums, g + 1)
                        A.activation(sroot, ssq, ACT.Sqrt).then_inc(d.root, 1)
                silu(12 * g + 11)
                for tp in range(2):
                    for t in (2 * tp, 2 * tp + 1):
                        act.wait_ge(d.rows_sum, T * g + t + 1)
                        for h in range(H4):
                            last = A.activation(Yt[:, t, h * P:(h + 1) * P], Pm[:, t % 2, h * P:(h + 1) * P], ACT.Exp,
                                                bias=nG[:, t, 4 * g + h:4 * g + h + 1])
                        last.then_inc(d.decay, 1)
                    for s in range(LEVELS - 1):
                        for w in range(2):
                            act.wait_ge(d.y_psum, y_no(g, tp, s, w))
                            A.copy(Yt[:, 2 * tp + w, :], ps[:, 4 + w, :]).then_inc(d.y_sb, 1)
                for t in range(T):
                    c = T * g + t
                    if t:
                        act.wait_ge(d2.ks, 3 * g + t)
                        act.wait_ge(d2.o, c)
                        for h in range(H4):
                            last = A.activation(qs[:, h * P:(h + 1) * P], ps[:, 1, h * P:(h + 1) * P], ACT.Copy,
                                                scale=eG[:, t, 4 * g + h:4 * g + h + 1])
                        last.then_inc(d2.qs, 1)
                    bank_done(act, d2.z, g, 3, f + 4 * g + 3, t)
                    A.activation(At[:, t, :], ps[:, 6 + t % 2, :], ACT.Silu).then_inc(d2.z_silu, 1)
                act.wait_ge(d2.hmean, g + 1)
                A.activation(hroot[:, 0:16], hmean[:, 0:16], ACT.Sqrt).then_inc(d2.hroot, 1)
                if g == 0:
                    act.wait_ge(d.x_spilled, 16 * T)
                for t in range(T):
                    act.wait_ge(d2.o_turned, T * g + t + 1)
                    A.copy(as_cols(place["odd"][0])[:, 4 * g:4 * g + 4, t * P:(t + 1) * P], bank(t % 2)).then_inc(d2.o_cols, 1)

        def odd_dve(dve, step, add_mixed):
            f = first["odd"]
            V = nc.vector
            dve.wait_ge(d.gates_psum, 1)
            step(V.tensor_copy(cw, ps[:, 7, 0:96]))
            ab = ps[:, 6, 0:64].rearrange("p (t n) -> p t n", n=16)
            V.tensor_tensor(ga, ab[:, :, 0:8], under(dt_b, T), ALU.add)
            V.tensor_copy(gb, ab[:, :, 8:16]).then_inc(d.gates_in, 1)
            dve.wait_ge(d.gates_ln, 1)
            step(V.scalar_tensor_tensor(out=gln, in0=ga, scalar=0.0, in1=gln, op0=ALU.max, op1=ALU.add))
            step(V.tensor_scalar(gbe, gbe, 1.0, None, ALU.add))
            step(V.reciprocal(beta, gbe))
            V.scalar_tensor_tensor(out=gg, in0=gln, scalar=-1.0, in1=under(ealog, T), op0=ALU.mult,
                                   op1=ALU.mult).then_inc(d.g_ready, 1)
            dve.wait_ge(d.sums_psum, 1)
            tot = ps[:, 6, 0:64].rearrange("p (a t h) -> p a t h", a=2, t=T)
            V.tensor_copy(Gs, tot[:, 0])
            step(V.tensor_copy(Gl, tot[:, 1]))
            V.tensor_scalar(nG, Gs, -1.0, None, ALU.mult)
            V.tensor_tensor(dG, Gl, Gs, ALU.subtract).then_inc(d.cums, 1)
            dve.wait_ge(d.gates_exp, 1)
            step(V.tensor_scalar(neG, eG, -1.0, None, ALU.mult))

            def taps(u):
                g, j, h = PU[u]
                dve.wait_ge(d.conv, u + 1)
                for s in range(1, CONV):
                    w = cw[:, 24 * (CONV - 1 - s) + 8 * j + 4 * g + h:24 * (CONV - 1 - s) + 8 * j + 4 * g + h + 1]
                    last = V.scalar_tensor_tensor(out=cv[:, u % 2, s:], in0=ps[:, u % 3, 0:N - s], scalar=w,
                                                  in1=cv[:, u % 2, s:], op0=ALU.mult, op1=ALU.add)
                    if s < CONV - 1:
                        step(last)
                last.then_inc(d.taps, 1)

            def tokens(u):
                g, j, h = PU[u]
                dve.wait_ge(d.posted, u + 1)
                if j:
                    w = 8 * g + 4 * (j - 1) + h
                    V.tensor_copy((ktok if j == 1 else vtok)[:, :, h * P:(h + 1) * P], bank(3 + w % 2)).then_inc(d.tok, 1)
                    dve.wait_ge(d.tok, w + 1)

            def squares(g):
                step(V.tensor_scalar(ssq[:, 0:16], ps[:, 5, 0:16], EPS, None, ALU.add))
                for t in range(T):
                    step(V.tensor_tensor(St.rearrange("p h d -> p (h d)"), ktok[:, t, :], ktok[:, t, :], ALU.mult))
                    step(V.tensor_reduce(srec[:, 4 * t:4 * t + 4], St, AX.X, ALU.add))
                V.tensor_scalar(ssq[:, 16:32], srec[:, 0:16], EPS, None, ALU.add).then_inc(d.sums, 1)

            def unit_keys(g):
                dve.wait_ge(d.root, g + 1)
                step(V.reciprocal(srec, sroot))
                step(V.tensor_scalar(srec[:, 0:16], srec[:, 0:16], float(P) ** -0.5, None, ALU.mult))
                for t in range(T):
                    rows = ktok[:, t, :].rearrange("p (h d) -> p h d", h=H4)
                    last = V.tensor_tensor(rows, rows, over(srec[:, 16 + 4 * t:20 + 4 * t], P), ALU.mult)
                last.then_inc(d.unit, 1)

            def key_columns(g, h):
                dve.wait_ge(d.back, H4 * g + h + 1)
                V.tensor_copy(kTh[:, h, :], ps[:, 6 + h % 2, :]).then_inc(d.cols, 1)

            for g in range(2):
                for u in range(12 * g, 12 * g + 12):
                    taps(u)
                    if u > 12 * g:
                        tokens(u - 1)
                    if u == 12 * g + 8:
                        squares(g)
                    if u == 12 * g + 9:
                        unit_keys(g)
                    if u >= 12 * g + 10:
                        key_columns(g, 2 * (u - 12 * g - 10))
                        key_columns(g, 2 * (u - 12 * g - 10) + 1)
                tokens(12 * g + 11)
                for tp in range(2):
                    for w in range(2):
                        t = 2 * tp + w
                        V.tensor_tensor(Pm[:, w, :].rearrange("p (h i) -> p h i", h=H4), under(upto, H4),
                                        over(gg[:, t, 4 * g:4 * g + 4], P), ALU.mult).then_inc(d.rows_in, 1)
                    for w in range(2):
                        c = T * g + 2 * tp + w
                        dve.wait_ge(d.rows_psum, c + 1)
                        V.tensor_tensor(Pm[:, w, :].rearrange("p (h i) -> p h i", h=H4), bank(w), under(decay0, H4),
                                        ALU.add).then_inc(d.rows_sum, 1)
                    for w in range(2):
                        t = 2 * tp + w
                        c = T * g + t
                        dve.wait_ge(d.decay, c + 1)
                        dve.wait_ge(d.grams, c + 1)
                        for h in range(H4):
                            V.scalar_tensor_tensor(out=LT[:, w, h * P:(h + 1) * P], in0=ps[:, 2 + w, h * P:(h + 1) * P],
                                                   scalar=beta[:, t, 4 * g + h:4 * g + h + 1], in1=Yt[:, t, h * P:(h + 1) * P],
                                                   op0=ALU.mult, op1=ALU.mult)
                        V.tensor_tensor(At[:, t, :], ps[:, 4 + w, :], Yt[:, t, :], ALU.mult).then_inc(d.xy, 1)
                    for s in range(LEVELS):
                        for w in range(2):
                            dve.wait_ge(d.p_psum, p_no(g, tp, s, w))
                            V.tensor_tensor(Pm[:, w, :].rearrange("p (h i) -> p h i", h=H4), bank(w),
                                            under(level[:, s, :], H4), ALU.mult).then_inc(d.p_sb, 1)
                        for w in range(2):
                            x, y = Xm[:, w, :], Yt[:, 2 * tp + w, :]
                            if s == 0:
                                dve.wait_ge(d.p_sb, p_no(g, tp, s, w))
                                V.tensor_tensor(x.rearrange("p (h i) -> p h i", h=H4), under(ident[:, :], H4),
                                                Pm[:, w, :].rearrange("p (h i) -> p h i", h=H4), ALU.subtract).then_inc(d.xy, 1)
                                continue
                            dve.wait_ge(d.xp, wp_no(g, tp, s, w))
                            dve.wait_ge(d.xy, xy_no(g, tp, s, w))
                            if s < LEVELS - 1:
                                V.tensor_tensor(x, x, ps[:, 2 + w, :], ALU.subtract).then_inc(d.xy, 1)
                            else:
                                V.tensor_tensor(y, y, ps[:, 4 + w, :], ALU.subtract).then_inc(d.xy, 1)
                for t in range(T):
                    c = T * g + t
                    cols = slice(4 * g, 4 * g + 4)
                    hd = "p (h e) -> p h e"
                    if t:
                        dve.wait_ge(d2.ks, 3 * g + t)
                        for h in range(H4):
                            last = V.scalar_tensor_tensor(out=Rr[:, h * P:(h + 1) * P], in0=ps[:, 0, h * P:(h + 1) * P],
                                                          scalar=neG[:, t, 4 * g + h:4 * g + h + 1],
                                                          in1=vtok[:, t, h * P:(h + 1) * P], op0=ALU.mult, op1=ALU.add)
                        last.then_inc(d2.r, 1)
                    dve.wait_ge(d2.tr, c + 1)
                    step(V.tensor_tensor(vn.rearrange(hd, h=H4), bank(2), over(beta[:, t, cols], P), ALU.mult))
                    V.tensor_tensor(vd.rearrange(hd, h=H4), vn.rearrange(hd, h=H4), over(eD[:, t, cols], P),
                                    ALU.mult).then_inc(d2.vn, 1)
                    if t < T - 1:
                        dve.wait_ge(d2.kv, 3 * g + t + 1)
                        if t == 0:
                            V.tensor_copy(St.rearrange("p h d -> p (h d)"), ps[:, 4, :]).then_inc(d2.st, 1)
                        else:
                            for h in range(H4):
                                last = V.scalar_tensor_tensor(out=St[:, h, :], in0=St[:, h, :],
                                                              scalar=eGl[:, t, 4 * g + h:4 * g + h + 1],
                                                              in1=ps[:, 4, h * P:(h + 1) * P], op0=ALU.mult, op1=ALU.add)
                            last.then_inc(d2.st, 1)
                        dve.wait_ge(d2.st, 3 * g + t + 1)
                    dve.wait_ge(d2.av, c + 1)
                    rows = vtok[:, t, :].rearrange(hd, h=H4)
                    if t:
                        dve.wait_ge(d2.qs, 3 * g + t)
                        step(V.tensor_tensor(rows, bank(3), qs.rearrange(hd, h=H4), ALU.add))
                        V.tensor_tensor(rows, rows, over(srec[:, 4 * t:4 * t + 4], P), ALU.mult).then_inc(d2.o, 1)
                    else:
                        V.tensor_tensor(rows, bank(3), over(srec[:, 0:4], P), ALU.mult).then_inc(d2.o, 1)
                    dve.wait_ge(d2.o, c + 1)
                for t in range(T):
                    step(V.tensor_tensor(Rr, vtok[:, t, :], vtok[:, t, :], ALU.mult))
                    step(V.tensor_reduce(hm[:, 4 * t:4 * t + 4], Rr.rearrange("p (h e) -> p h e", h=H4), AX.X, ALU.add))
                V.tensor_scalar(hmean[:, 0:16], hm[:, 0:16], 1.0 / P, EPS, ALU.mult, ALU.add).then_inc(d2.hmean, 1)
                dve.wait_ge(d2.hroot, g + 1)
                step(V.reciprocal(hrec[:, 0:16], hroot[:, 0:16]))
                for t in range(T):
                    rows = vtok[:, t, :].rearrange("p (h e) -> p h e", h=H4)
                    step(V.tensor_tensor(rows, rows, over(hrec[:, 4 * t:4 * t + 4], P), ALU.mult))
                    step(V.tensor_tensor(rows, rows, under(gn, H4), ALU.mult))
                    dve.wait_ge(d2.z_silu, T * g + t + 1)
                    V.tensor_tensor(vtok[:, t, :], vtok[:, t, :], At[:, t, :], ALU.mult).then_inc(d2.on, 1)
            dve.wait_ge(d2.x_back, 16 * T)
            add_mixed(place["odd"][1], d2.mixed, "odd", 8)

        @block.sync
        def _(sp):
            def load_chunk(k, dst, src):
                if k >= RING:
                    sp.wait_ge(al.chunk_used, k - RING + 1)
                sp.dma_start(dst, src).then_inc(landed[slot(k)], 16)

            def load_columns(k, w, col):
                load_chunk(k, chunk(k), w[:, col:col + N].rearrange("(p c) n -> p c n", c=KC))

            def expert_load(s, i, j, e):
                L = int(s[3])
                for n, name in enumerate(("expert_w_gate", "expert_w_up", "expert_w_down")):
                    k = first[s] + 3 * j + n
                    if not isinstance(i, int) or i * RING + k >= RING:
                        sp.wait_ge(al.chunk_used, i * RING + (k - RING + 1))
                    src = io[name][L, e].rearrange("(p c) f -> p (c f)", p=P)
                    sp.dma_start(ring[:, slot(k), :], src).then_inc(landed[slot(k)], 16)

            def router(L):
                sp.dma_start(wr[:, :, 0:NG], io["router_group_w"][L].rearrange("(p c) g -> p c g", c=KC)).then_inc(r.gates, 16)
                for q in range(NG):
                    sp.dma_start(wr[:, :, NG + q * EPG:NG + (q + 1) * EPG],
                                 io["router_expert_w"][L, q].rearrange("(p c) e -> p c e", c=KC)).then_inc(r.gates, 16)
                sp.dma_start(rbias[:, 0:NG], io["router_group_b"][L].partition_broadcast(P)).then_inc(r.gates, 16)
                sp.dma_start(rbias[:, NG:NG + NE],
                             io["router_expert_b"][L].rearrange("g e -> (g e)").partition_broadcast(P)).then_inc(r.gates, 16)

            def moe(s):
                L, v = int(s[3]), moe_turn[s]
                for t in range(T):
                    sp.wait_ge(nm.rows, order_of[s] * T + t + 1)
                    sp.dma_start(h_dram[L][t * P:(t + 1) * P, :], xn[:, t, :]).then_inc(r.h_stored, 16)
                with sp.Fori(1, PER) as i:
                    for j in range(2):
                        expert_load(s, i, j, i * 2 + j)
                if v + 1 < len(moe_turn):
                    sp.wait_ge(r.counted, v + 1)
                    router(L + 1)
                overflow(s)

            def overflow(s):
                L = int(s[3])
                f = ov[L]
                sp.wait_ge(r.tables, moe_turn[s] + 1)
                most = sp.value_load(count_i[0:1, int(s[3]), NE:NE + 1], min_val=0, max_val=S)
                with sp.If(most > SLOTS):
                    sp.wait_ge(al.chunk_used, first[s] + 3 * NE)
                    for b in range(1, SLOT_BLOCKS):
                        with sp.If(most > b * SLOTS), sp.Fori(0, NE) as q:
                            n = q + (b - 1) * NE
                            for c, name in enumerate(("expert_w_gate", "expert_w_up", "expert_w_down")):
                                sp.dma_start(ring[:, c, :], io[name][L, q].rearrange("(p c) f -> p (c f)", p=P)
                                             ).then_inc(f.load, 16)
                            sp.wait_ge(f.scatter, n * 16 + 16)
                            sp.sem_inc(f.load, 1)

            def combine(s):
                v, L = moe_turn[s], int(s[3])
                for b in range(2):
                    sp.wait_ge(scattered[b], 16 * PER * (v + 1))
                src = y_dram[L].rearrange("(t p k) d -> t p (k d)", t=T, k=2)
                for t in range(T):
                    sp.dma_start(yc[:, t, :], src[t]).then_inc(back[t], 16)

            for t in range(T):
                sp.dma_start(as_tiles(buf0)[:, t, :], io["x"][0, t * P:(t + 1) * P, :]).then_inc(x_landed[t], 16)
            sp.dma_start(ident[:, :], io["c_ident"]).then_inc(al.const, 16)
            sp.dma_start(iota[:, :], io["c_iota"]).then_inc(al.const, 16)
            for q, a in enumerate((io["even_attn_norm"][0], io["ffn_norm"][0], io["odd_attn_norm"][0], io["ffn_norm"][1])):
                sp.dma_start(gcols[:, q, :], a.rearrange("(p c) -> p c", c=KC)).then_inc(al.const, 16)
            sp.dma_start(out_gain, io["b_out_norm"][0].partition_broadcast(P)).then_inc(al.const, 16)
            if moe_turn:
                for dst, n in ((before, "c_before"), (value, "c_value"), (far, "c_far")):
                    sp.dma_start(dst[:], io[n]).then_inc(r.gates, 16)
                router(int(min(moe_turn)[3]))

            def prefetch(s, half=None):
                chunks = range(RING) if half is None else range(3 * half, 3 * half + 3)
                if s == "even":
                    for b in chunks:
                        load_columns(first[s] + b, io["even_w_in"][0], b * N)
                elif s == "odd":
                    odd_prefetch(load_columns, chunks)
                else:
                    for j in range(2) if half is None else (half,):
                        expert_load(s, 0, j, j)

            for i, s in enumerate(stages):
                if i == 0:
                    if s == "even":
                        for q, n in enumerate(("a_q_norm", "a_k_norm", "b_q_norm", "b_k_norm")):
                            sp.dma_start(qk_gain[:, q, :], io[n][0].partition_broadcast(P)).then_inc(e.tables, 16)
                        for q, n in enumerate(("b_lambda_q1", "b_lambda_k1", "b_lambda_q2", "b_lambda_k2")):
                            sp.dma_start(lam_in[:, q, :], io[n][0].rearrange("h d -> (h d)").partition_broadcast(P)
                                         ).then_inc(e.tables, 16)
                        for dst, n in ((cos2, "c_cos"), (sin2, "c_sin"), (dilated, "c_dilated"), (causal, "c_causal")):
                            sp.dma_start(dst, io[n]).then_inc(e.tables, 16)
                    if s == "odd":
                        odd_tables(sp)
                    prefetch(s)
                if s == "even":
                    for n in range(2):
                        load_columns(first[s] + 6 + n, io["even_w_out"][0], n * N)
                elif s == "odd":
                    odd_sp(sp, load_chunk, load_columns)
                else:
                    moe(s)
                after = stages[i + 1:i + 2]
                if s in moe_turn:
                    for a in after:
                        prefetch(a, 0)
                    combine(s)
                    for a in after:
                        if a == "odd":
                            odd_tables(sp)
                        prefetch(a, 1)
                else:
                    for a in after:
                        prefetch(a)
            for t in range(T):
                sp.wait_ge(al.x_tiles, tiles - n_tiles[stages[-1]] + (t + 1 if stages[-1][:3] == "moe" else T + t + 1))
                sp.dma_start(out[0, t * P:(t + 1) * P, :], as_tiles(x_last)[:, t, :]).then_inc(al.stored, 16)
            sp.wait_ge(al.stored, 16 * T)

        @block.scalar
        def _(act):
            step = Order(act, in_act)

            def norm(s):
                x, o = as_tiles(place[s][0]), order_of[s]
                for t in range(T):
                    if o:
                        act.wait_ge(al.x_tiles, x_need[s] - T + t + 1)
                    else:
                        act.wait_ge(x_landed[t], 16)
                    nc.scalar.activation(xn[:, t, :], x[:, t, :], ACT.Square,
                                         accum_out=sumsq[:, t:t + 1]).then_inc(nm.squares, 1)
                    act.wait_ge(nm.meansq, o * T + t + 1)
                    nc.scalar.activation(rootsq[:, t:t + 1], meansq[:, t:t + 1], ACT.Sqrt).then_inc(nm.root, 1)

            def even():
                f = first["even"]
                act.wait_ge(e.lam_exp, 1)
                nc.scalar.activation(lam4[:, 8:16], lam4[:, 0:8], ACT.Exp).then_inc(e.lam, 1)
                for k, t in PROJ:
                    if k not in QK_NO:
                        continue
                    w = QK_NO[k] * T + t
                    u = T * k + t
                    bank_done(act, e.proj, k, 3, f + k, t)
                    if w:
                        act.wait_ge(e.sums, w)
                    nc.scalar.activation(sq, ps[:, u % 4, :], ACT.Square).then_inc(e.squared, 1)
                    act.wait_ge(e.mean, w + 1)
                    nc.scalar.activation(root8, mean8, ACT.Sqrt).then_inc(e.root, 1)
                for i, (blk, pair, a, half) in enumerate(UNITS):
                    nk = (a + 1) * P
                    act.wait_ge(e.negmax, i + 1)
                    if i >= 2:
                        act.wait_ge(e.p_turned, i - 1)
                    nc.scalar.activation(pr[:, i % 2, 0:nk], sm[:, i % 2, 0:nk], ACT.Exp, bias=neg_max[:, i:i + 1],
                                         accum_out=den[:, i:i + 1]).then_inc(e.probs, 1)
                act.wait_ge(e.head_mean, 1)
                nc.scalar.activation(head16[:, 32:48], head16[:, 16:32], ACT.Sqrt).then_inc(e.head_root, 1)
                for i in range(2 * T):
                    act.wait_ge(e.o_turned, i + 1)
                    t, q = i // 2, i % 2
                    nc.scalar.copy(oT[:, 4 * q:4 * q + 4, t * P:(t + 1) * P], bank(i % 4)).then_inc(e.o_cols, 1)

            def expert(s, i, b):
                n = 2 * i + (b + NE * moe_turn[s])
                k = first[s] + 3 * b
                act.wait_ge(al.chunk_used, i * RING + k + 2)
                nc.scalar.activation(sg[:, b, :], ps[0:SLOTS, 2, :], ACT.Silu).then_inc(m.silu, 1)
                act.wait_ge(m.h_turned, n + 1)
                nc.scalar.copy(hidT[:, b, :], ps[:, 4, 0:FF // P * SLOTS]).then_inc(m.h_cols, 1)
                act.wait_ge(m.down, n + 1)
                if not isinstance(i, int) or i + moe_turn[s] > 0:
                    act.wait_ge(scattered[b], i * 16 + 16 * PER * moe_turn[s])
                nc.scalar.copy(yb[:, b, 0:N], ps[0:SLOTS, 5, :]).then_inc(m.y_left, 1)

            def moe(s):
                v = moe_turn[s]
                act.wait_ge(r.exp_in, 2 * v + 1)
                nc.scalar.activation(rt[:, 11, 0:T * NG], rt[:, 10, 0:T * NG], ACT.Exp).then_inc(r.exp_out, 1)
                act.wait_ge(r.exp_in, 2 * v + 2)
                nc.scalar.activation(w_mix[:, 1, :], w_mix[:, 0, :], ACT.Exp).then_inc(r.exp_out, 1)
                for b in range(2):
                    expert(s, 0, b)
                with act.Fori(1, PER) as i:
                    for b in range(2):
                        expert(s, i, b)
                over(s)

            def over(s):
                f = ov[int(s[3])]
                most = act.value_load(count_i[0:1, int(s[3]), NE:NE + 1], min_val=0, max_val=S)
                with act.If(most > SLOTS):
                    for b in range(1, SLOT_BLOCKS):
                        with act.If(most > b * SLOTS), act.Fori(0, NE) as q:
                            n = q + (b - 1) * NE
                            act.wait_ge(f.pe, n * 4 + 2)
                            nc.scalar.activation(sg[:, 0, :], ps[0:SLOTS, 2, :], ACT.Silu).then_inc(f.act, 1)

            for s in stages:
                norm(s)
                if s == "even":
                    even()
                elif s == "odd":
                    odd_act(act, step)
                else:
                    moe(s)

        @block.tensor
        def _(pe):
            def turn(dst, rows, q):
                v, n = rows.rearrange("p (m c) -> p c m", c=KC), rows.shape[0]
                for j in range(4):
                    last = nc.tensor.transpose(ps[:, dst, j * n:(j + 1) * n], v[:, 4 * q + j, :], ident[0:n, 0:n])
                return last

            def norm(s):
                o = order_of[s]
                if o == 0:
                    pe.wait_ge(al.const, CONSTS)
                for i in range(2 * T):
                    pe.wait_ge(nm.rows, o * T + i // 2 + 1)
                    if i >= 4:
                        pe.wait_ge(nm.cols, o * 2 * T + i - 3)
                    turn(i % 4, xn[:, i // 2, :], i % 2).then_inc(nm.turned, 1)
                pe.wait_ge(nm.cols, (o + 1) * 2 * T)

            def even():
                ht, f = as_cols(place["even"][1]), first["even"]

                def project(k, t):
                    u = T * k + t
                    if t == 0:
                        wait_chunk(pe, f + k)
                    if u >= 4:
                        pe.wait_ge(e.taken, u - 3)
                    for c in range(KC):
                        last = nc.tensor.matmul(ps[:, u % 4, :], ht[:, c, t * P:(t + 1) * P], chunk(f + k)[:, c, :],
                                                start=(c == 0), stop=(c == KC - 1))
                    last.then_inc(al.chunk_used if t == T - 1 else e.proj, 1)

                def turn_qk(w):
                    pe.wait_ge(e.rotated, w + 1)
                    if w >= 2:
                        pe.wait_ge(e.qk_cols, w - 1)
                    for j in range(4):
                        last = nc.tensor.transpose(ps[:, 4 + w % 2, j * P:(j + 1) * P],
                                                   rot[:, w % 2, j * P:(j + 1) * P], ident[:, :])
                    last.then_inc(e.turned, 1)

                behind = None
                for k, t in PROJ:
                    project(k, t)
                    if behind is not None:
                        turn_qk(behind)
                    behind = QK_NO[k] * T + t if k in QK_NO else None
                pe.wait_ge(e.qk_cols, 16)
                pe.wait_ge(e.taken, 24)

                def scores(i):
                    blk, pair, a, half = UNITS[i]
                    q0 = 0 if blk == "A" else 8
                    rows = slice(half * HEAD, half * HEAD + HEAD)
                    if i >= 2:
                        pe.wait_ge(e.masked, i - 1)
                    nc.tensor.matmul(ps[:, i % 2, 0:(a + 1) * P], qkT[rows, q0 + pair, a * P:(a + 1) * P],
                                     qkT[rows, q0 + 4 + pair, 0:(a + 1) * P], start=True, stop=True).then_inc(e.scores, 1)

                def turn_probs(i):
                    a = UNITS[i][2]
                    pe.wait_ge(e.probs, i + 1)
                    if i >= 2:
                        pe.wait_ge(e.p_cols, i - 1)
                    for j in range(a + 1):
                        last = nc.tensor.transpose(ps[:, 2 + i % 2, j * P:(j + 1) * P],
                                                   pr[:, i % 2, j * P:(j + 1) * P], ident[:, :])
                    last.then_inc(e.p_turned, 1)

                def weigh(i):
                    blk, pair, a, half = UNITS[i]
                    pe.wait_ge(e.p_cols, i + 1)
                    if i >= 2:
                        pe.wait_ge(e.normed, i - 1)
                    for j in range(a + 1):
                        if blk == "A":
                            v = av[:, j, (2 * pair + half) * HEAD:(2 * pair + half + 1) * HEAD]
                        else:
                            v = bv[:, j, pair * P:(pair + 1) * P]
                        last = nc.tensor.matmul(ps[:, 4 + i % 2, 0:v.shape[1]], pT[:, i % 2, j * P:(j + 1) * P], v,
                                                start=(j == 0), stop=(j == a))
                    last.then_inc(e.pv, 1)

                for i in range(len(UNITS) + 2):
                    if i < len(UNITS):
                        scores(i)
                    if 1 <= i <= len(UNITS):
                        turn_probs(i - 1)
                    if i >= 2:
                        weigh(i - 2)

                attn = as_tiles(place["even"][1])
                for i in range(2 * T):
                    pe.wait_ge(e.normed, len(UNITS) + i // 2 + 1)
                    if i >= 4:
                        pe.wait_ge(e.o_cols, i - 3)
                    turn(i % 4, attn[:, i // 2, :], i % 2).then_inc(e.o_turned, 1)
                pe.wait_ge(e.o_cols, 2 * T)
                for n in range(2):
                    for t in range(T):
                        u = T * n + t
                        if t == 0:
                            wait_chunk(pe, f + 6 + n)
                        if u >= 4:
                            pe.wait_ge(al.x_tiles, x_need["even"] + u - 3)
                        for c in range(KC):
                            last = nc.tensor.matmul(ps[:, 4 + u % 4, :], oT[:, c, t * P:(t + 1) * P],
                                                    chunk(f + 6 + n)[:, c, :], start=(c == 0), stop=(c == KC - 1))
                        last.then_inc(al.chunk_used if t == T - 1 else e.mixed, 1)

            def side_by_side(b, xT, w, k):
                last = [None, None]
                for c in range(k):
                    for q in range(2):
                        last[q] = nc.tensor.matmul(ps[q * SLOTS:(q + 1) * SLOTS, b + q, :],
                                                   xT[:, c * SLOTS:(c + 1) * SLOTS], w[q][:, c, :],
                                                   start=(c == 0), stop=(c == k - 1))
                return last

            def turn_hidden(b):
                rows = hid[:, b, :].rearrange("p (m c) -> p c m", c=FF // P)
                for j in range(FF // P):
                    last = nc.tensor.transpose(ps[:, 4, j * SLOTS:(j + 1) * SLOTS], rows[:, j, :],
                                               ident[0:SLOTS, 0:SLOTS])
                return last

            def waited():
                pe.sem_inc(al.passed, 1)

            def turn_x(s, i, b):
                v = moe_turn[s]
                n = 2 * i + (b + NE * v)
                pe.wait_ge(gathered[b], i * 16 + 16 * (1 + PER * v))
                for q in range(2):
                    if not isinstance(n, int) or n:
                        pe.wait_ge(m.x_cols, 2 * n + (q - 1))
                    waited()
                    turn(q, xg[:, b, :], q).then_inc(m.x_turned, 1)

            def expert(s, i, b, last_one=False):
                v, k = moe_turn[s], first[s] + 3 * b
                n = 2 * i + (b + NE * v)
                pe.wait_ge(m.x_cols, 2 * n + 2)
                wait_chunk(pe, k, i)
                wait_chunk(pe, k + 1, i)
                if not isinstance(n, int) or n:
                    pe.wait_ge(m.hidden, n)
                for last in side_by_side(2, xgT[:, b, :], (chunk(k), chunk(k + 1)), KC):
                    last.then_inc(al.chunk_used, 1)
                if not last_one:
                    turn_x(s, i + b, 1 - b)
                pe.wait_ge(m.hidden, n + 1)
                if not isinstance(n, int) or n:
                    pe.wait_ge(m.h_cols, n)
                waited()
                turn_hidden(b).then_inc(m.h_turned, 1)
                wait_chunk(pe, k + 2, i)
                pe.wait_ge(m.h_cols, n + 1)
                if not isinstance(n, int) or n:
                    pe.wait_ge(m.y_left, n)
                    pe.wait_ge(m.y_right, n)
                w = chunk(k + 2, FF // P)
                left, right = side_by_side(5, hidT[:, b, :], (w[:, :, 0:N], w[:, :, N:D]), FF // P)
                left.then_inc(m.down, 1)
                right.then_inc(al.chunk_used, 1)

            def slot_table():
                for i in range(2 * T):
                    last = nc.tensor.matmul(ps[0:SLOTS, 7, 0:2 * NE], slot_hot[:, i, :], values[:, i, :],
                                            start=(i == 0), stop=(i == 2 * T - 1))
                return last

            def moe(s):
                v = moe_turn[s]
                ht = as_cols(place[s][1])
                pe.wait_ge(r.gates, 16 * (7 * v + 10))
                for t in range(T):
                    for c in range(KC):
                        last = nc.tensor.matmul(ps[:, 4, t * 36:(t + 1) * 36], ht[:, c, t * P:(t + 1) * P],
                                                wr[:, c, :], start=(c == 0), stop=(c == KC - 1))
                last.then_inc(r.logits, 1)
                pe.wait_ge(r.counted, v + 1)
                chosen = rt[:, 9, :].rearrange("p (t e) -> p t e", t=T)
                for t in range(T):
                    for q in range(t + 1):
                        nc.tensor.matmul(ps[:, 5, t * NE:(t + 1) * NE], before[:, :] if q == t else ones[:, :],
                                         chosen[:, q, :], start=(q == 0), stop=(q == t))
                for q in range(T):
                    last = nc.tensor.matmul(ps[:, 6, 0:NE], ones[:, :], chosen[:, q, :], start=(q == 0), stop=(q == T - 1))
                last.then_inc(r.placed, 1)
                pe.wait_ge(r.slots, v + 1)
                slot_table().then_inc(r.tables_psum, 1)
                turn_x(s, 0, 0)
                for b in range(2):
                    expert(s, 0, b)
                with pe.Fori(1, PER - 1) as i:
                    for b in range(2):
                        expert(s, i, b)
                for b in range(2):
                    expert(s, PER - 1, b, last_one=(b == 1))
                over(s)

            def over(s):
                f = ov[int(s[3])]
                most = pe.value_load(count_i[0:1, int(s[3]), NE:NE + 1], min_val=0, max_val=S)
                with pe.If(most > SLOTS):
                    for b in range(1, SLOT_BLOCKS):
                        with pe.If(most > b * SLOTS):
                            pe.wait_ge(f.hot, b)
                            slot_table().then_inc(f.tab, 1)
                            with pe.Fori(0, NE) as q:
                                n = q + (b - 1) * NE
                                pe.wait_ge(f.gather, n * 16 + 16)
                                waited()
                                for h in range(2):
                                    last = turn(h, xg[:, 0, :], h)
                                last.then_inc(f.pe, 1)
                                pe.wait_ge(f.dve, n * 6 + 2)
                                pe.wait_ge(f.load, n * 49 + 48)
                                side_by_side(2, xgT[:, 0, :], (chunk(0), chunk(1)), KC)[1].then_inc(f.pe, 1)
                                pe.wait_ge(f.dve, n * 6 + 3)
                                waited()
                                turn_hidden(0).then_inc(f.pe, 1)
                                pe.wait_ge(f.dve, n * 6 + 4)
                                w = chunk(2, FF // P)
                                side_by_side(5, hidT[:, 0, :], (w[:, :, 0:N], w[:, :, N:D]), FF // P)[1].then_inc(f.pe, 1)

            for s in stages:
                norm(s)
                if s == "even":
                    even()
                elif s == "odd":
                    odd_pe(pe)
                else:
                    moe(s)

        @block.vector
        def _(dve):
            step = Order(dve, in_dve)
            V = nc.vector

            def norm(s):
                x, ht, o = as_tiles(place[s][0]), as_cols(place[s][1]), order_of[s]
                for t in range(T):
                    one = slice(t, t + 1)
                    dve.wait_ge(nm.squares, o * T + t + 1)
                    V.tensor_scalar(meansq[:, one], sumsq[:, one], 1.0 / D, EPS, ALU.mult, ALU.add).then_inc(nm.meansq, 1)
                    dve.wait_ge(nm.root, o * T + t + 1)
                    step(V.reciprocal(rstd[:, one], rootsq[:, one]))
                    V.tensor_scalar(xn[:, t, :], x[:, t, :], rstd[:, t:t + 1], None, ALU.mult).then_inc(nm.rows, 1)
                if o == 0:
                    dve.wait_ge(al.const, CONSTS)
                for i in range(2 * T):
                    t, q = i // 2, i % 2
                    dve.wait_ge(nm.turned, o * 2 * T + i + 1)
                    gain = gcols[:, gain_no[s], 4 * q:4 * q + 4]
                    V.tensor_tensor(ht[:, 4 * q:4 * q + 4, t * P:(t + 1) * P], bank(i % 4), over(gain, P),
                                    ALU.mult).then_inc(nm.cols, 1)

            def even_tables():
                dve.wait_ge(e.tables, 16 * 12)
                for q in range(4):
                    by = 0.125 if q % 2 == 0 else 1.0
                    c = cg[:, q, :].rearrange("p (t h) -> p t h", t=T)
                    n = sgn[:, q, :].rearrange("p (t h) -> p t h", t=T)
                    V.scalar_tensor_tensor(out=c, in0=cos2, scalar=by, in1=under(qk_gain[:, q, :], T),
                                           op0=ALU.mult, op1=ALU.mult)
                    V.scalar_tensor_tensor(out=n[:, :, 0:32], in0=sin2[:, :, 0:32], scalar=by,
                                           in1=under(qk_gain[:, q, 32:64], T), op0=ALU.mult, op1=ALU.mult)
                    step(V.scalar_tensor_tensor(out=n[:, :, 32:64], in0=sin2[:, :, 32:64], scalar=by,
                                                in1=under(qk_gain[:, q, 0:32], T), op0=ALU.mult, op1=ALU.mult))
                for q in range(2):
                    step(V.tensor_tensor(t1[:, 0:256], lam_in[:, 2 * q, :], lam_in[:, 2 * q + 1, :], ALU.mult))
                    last = V.tensor_reduce(lam4[:, 4 * q:4 * q + 4], t1[:, 0:256].rearrange("p (h d) -> p h d", h=4),
                                           AX.X, ALU.add)
                    if q == 0:
                        step(last)
                last.then_inc(e.lam_exp, 1)
                dve.wait_ge(e.lam, 1)
                step(V.tensor_tensor(lam4[:, 16:20], lam4[:, 12:16], lam4[:, 8:12], ALU.subtract))
                step(V.tensor_scalar(lam4[:, 16:20], lam4[:, 16:20], -LAM_INIT, None, ALU.add))
                step(V.tensor_scalar(out_gain, out_gain, 1.0 - LAM_INIT, None, ALU.mult))

            def even():
                f = first["even"]
                even_tables()

                def qk_unit(k, t):
                    q, u = QK_NO[k], T * k + t
                    w = q * T + t
                    x = ps[:, u % 4, :].rearrange("p (h d) -> p h d", d=HEAD)
                    dve.wait_ge(e.squared, w + 1)
                    V.tensor_reduce(ms8, sq.rearrange("p (h d) -> p h d", d=HEAD), AX.X, ALU.add).then_inc(e.sums, 1)
                    dve.wait_ge(e.sums, w + 1)
                    V.tensor_scalar(mean8, ms8, 1.0 / HEAD, EPS, ALU.mult, ALU.add).then_inc(e.mean, 1)
                    dve.wait_ge(e.root, w + 1)
                    step(V.reciprocal(rstd8, root8))
                    qv, av_, bv_, rv = (z.rearrange("p (h d) -> p h d", d=HEAD) for z in (qn, t1, t2, rot[:, w % 2, :]))
                    V.tensor_tensor(qv, x, over(rstd8, HEAD), ALU.mult).then_inc(e.taken, 1)
                    dve.wait_ge(e.taken, u + 1)
                    c, n = cg[:, q, t * HEAD:(t + 1) * HEAD], sgn[:, q, t * HEAD:(t + 1) * HEAD]
                    V.tensor_tensor(av_, qv, under(c, 8), ALU.mult)
                    V.tensor_tensor(bv_[:, :, 0:32], qv[:, :, 32:64], under(n[:, 0:32], 8), ALU.mult)
                    step(V.tensor_tensor(bv_[:, :, 32:64], qv[:, :, 0:32], under(n[:, 32:64], 8), ALU.mult))
                    if w >= 2:
                        dve.wait_ge(e.turned, w - 1)
                    V.tensor_tensor(rot[:, w % 2, :], t1, t2, ALU.add).then_inc(e.rotated, 1)

                def qk_columns(w):
                    q, t = w // T, w % T
                    dve.wait_ge(e.turned, w + 1)
                    V.tensor_copy(qkT[:, 4 * q:4 * q + 4, t * P:(t + 1) * P], bank(4 + w % 2)).then_inc(e.qk_cols, 1)

                behind = None
                for k, t in PROJ:
                    bank_done(dve, e.proj, k, 3, f + k, t)
                    if k in QK_NO:
                        qk_unit(k, t)
                    else:
                        V.tensor_copy((av if k == 2 else bv)[:, t, :], ps[:, (T * k + t) % 4, :]).then_inc(e.taken, 1)
                    if behind is not None:
                        qk_columns(behind)
                    behind = QK_NO[k] * T + t if k in QK_NO else None

                def mask(i):
                    blk, pair, a, half = UNITS[i]
                    nk = (a + 1) * P
                    dve.wait_ge(e.scores, i + 1)
                    if i >= 2:
                        dve.wait_ge(e.probs, i - 1)
                    V.tensor_tensor_reduce(sm[:, i % 2, 0:nk], ps[:, i % 2, 0:nk],
                                           (dilated if blk == "A" else causal)[:, N - nk:N], 1.0, NEG,
                                           ALU.add, ALU.max, row_max[:, i:i + 1]).then_inc(e.masked, 1)
                    dve.wait_ge(e.masked, i + 1)
                    V.tensor_scalar(neg_max[:, i:i + 1], row_max[:, i:i + 1], -1.0, None, ALU.mult).then_inc(e.negmax, 1)

                def prob_columns(i):
                    nk = (UNITS[i][2] + 1) * P
                    dve.wait_ge(e.p_turned, i + 1)
                    if i >= 2:
                        dve.wait_ge(e.pv, i - 1)
                    V.tensor_copy(pT[:, i % 2, 0:nk], ps[:, 2 + i % 2, 0:nk]).then_inc(e.p_cols, 1)

                attn = as_tiles(place["even"][1])

                def normalise(i):
                    blk, pair, a, half = UNITS[i]
                    dve.wait_ge(e.pv, i + 1)
                    step(V.reciprocal(rden[:, i:i + 1], den[:, i:i + 1]))
                    acc, rd = ps[:, 4 + i % 2, :], rden[:, i:i + 1]
                    if blk == "A":
                        h = 2 * pair + half
                        last = V.tensor_scalar(attn[:, a, h * HEAD:(h + 1) * HEAD], acc[:, 0:HEAD], rd, None, ALU.mult)
                    elif half == 0:
                        last = V.tensor_scalar(o1, acc[:, 0:P], rd, None, ALU.mult)
                    else:
                        step(V.tensor_tensor(nlam, rd, lam4[:, 16 + pair:17 + pair], ALU.mult))
                        last = V.scalar_tensor_tensor(out=attn[:, a, N + pair * P:N + (pair + 1) * P], in0=acc[:, 0:P],
                                                      scalar=nlam, in1=o1, op0=ALU.mult, op1=ALU.add)
                    last.then_inc(e.normed, 1)
                    dve.wait_ge(e.normed, i + 1)

                for i in range(len(UNITS) + 2):
                    if i < len(UNITS):
                        mask(i)
                    if 1 <= i <= len(UNITS):
                        prob_columns(i - 1)
                    if i >= 2:
                        normalise(i - 2)

                for a in range(T):
                    step(V.tensor_tensor(t2, attn[:, a, N:D], attn[:, a, N:D], ALU.mult))
                    step(V.tensor_reduce(head16[:, 4 * a:4 * a + 4], t2.rearrange("p (h d) -> p h d", h=4), AX.X, ALU.add))
                V.tensor_scalar(head16[:, 16:32], head16[:, 0:16], 1.0 / P, EPS, ALU.mult, ALU.add).then_inc(e.head_mean, 1)
                dve.wait_ge(e.head_root, 1)
                step(V.reciprocal(head16[:, 48:64], head16[:, 32:48]))
                for a in range(T):
                    rows = attn[:, a, N:D].rearrange("p (h d) -> p h d", h=4)
                    step(V.tensor_tensor(rows, rows, over(head16[:, 48 + 4 * a:52 + 4 * a], P), ALU.mult))
                    V.tensor_tensor(rows, rows, under(out_gain, 4), ALU.mult).then_inc(e.normed, 1)
                add_mixed(place["even"][0], e.mixed, "even", 6)

            def add_mixed(xbuf, ready, s, c):
                x = as_tiles(xbuf)
                for n in range(2):
                    for t in range(T):
                        u = T * n + t
                        bank_done(dve, ready, n, 3, first[s] + c + n, t)
                        V.tensor_tensor(x[:, t, n * N:(n + 1) * N], x[:, t, n * N:(n + 1) * N], ps[:, 4 + u % 4, :],
                                        ALU.add).then_inc(al.x_tiles, 1)

            def pick(hot, scores, best):
                n = scores.shape[2]
                step(V.tensor_reduce(best, scores, AX.X, ALU.max))
                step(V.tensor_tensor(hot, scores, over(best, n), ALU.is_equal))
                step(V.scalar_tensor_tensor(out=hot, in0=hot, scalar=-1000.0, in1=under(iota[:, 0:n], T),
                                            op0=ALU.mult, op1=ALU.add))
                step(V.tensor_reduce(least, hot, AX.X, ALU.min))
                step(V.tensor_tensor(hot, hot, over(least, n), ALU.is_equal))

            def slot_rows():
                V.tensor_tensor(slot_hot[:, 0:T, :], under(iota[:, 0:SLOTS], T), over(p1, SLOTS), ALU.is_equal)
                return V.tensor_tensor(slot_hot[:, T:2 * T, :], under(iota[:, 0:SLOTS], T), over(p2, SLOTS), ALU.is_equal)

            def slot_indices(step):
                step(V.tensor_copy(tab, ps[0:SLOTS, 7, 0:2 * NE]))
                a, t, gone = tab[:, 0:NE], tab[:, NE:2 * NE], rt[0:SLOTS, 6, 0:NE]
                step(V.tensor_scalar(gone, a, 0.0, far[0:SLOTS, :], ALU.is_equal, ALU.mult))
                step(V.tensor_tensor(t, t, gone, ALU.add))
                step(V.scalar_tensor_tensor(out=a, in0=a, scalar=-1.0, in1=gone, op0=ALU.add, op1=ALU.add))
                V.tensor_copy(tab_u[:, 0, :], a)
                return V.tensor_copy(tab_u[:, 1, :], t)

            def route(s):
                v = moe_turn[s]

                def grid(i, n=NE):
                    return rt[:, i, 0:T * n].rearrange("p (t e) -> p t e", t=T)

                dve.wait_ge(r.logits, v + 1)
                step(V.tensor_tensor(lg, ps[:, 4, 0:T * 36].rearrange("p (t e) -> p t e", t=T), under(rbias[:, :], T), ALU.add))
                lgg, lge = lg[:, :, 0:NG], lg[:, :, NG:NG + NE]
                group, el, hot1, hot2 = grid(0, NG), grid(1), grid(2), grid(3)
                pick(group, lgg, gmax)
                V.tensor_tensor(grid(10, NG), lgg, over(gmax, NG), ALU.subtract).then_inc(r.exp_in, 1)
                step(V.tensor_scalar(grid(4, NG), group, -1.0, -NEG, ALU.add, ALU.mult))
                for q in range(NG):
                    last = V.tensor_tensor(el[:, :, q * EPG:(q + 1) * EPG], lge[:, :, q * EPG:(q + 1) * EPG],
                                           grid(4, NG)[:, :, q:q + 1].to_broadcast([P, T, EPG]), ALU.add)
                step(last)
                pick(hot1, el, m1)
                step(V.scalar_tensor_tensor(out=el, in0=hot1, scalar=2 * NEG, in1=el, op0=ALU.mult, op1=ALU.add))
                pick(hot2, el, m2)
                V.tensor_tensor(w_mix[:, 0, :], m2, m1, ALU.subtract).then_inc(r.exp_in, 1)
                chosen = grid(9)
                V.tensor_tensor(chosen, hot1, hot2, ALU.add).then_inc(r.counted, 1)
                dve.wait_ge(r.exp_out, 2 * v + 1)
                step(V.tensor_reduce(gsum, grid(11, NG), AX.X, ALU.add))
                step(V.reciprocal(gw, gsum))
                dve.wait_ge(r.exp_out, 2 * v + 2)
                step(V.tensor_scalar(p1, w_mix[:, 1, :], 1.0, None, ALU.add))
                step(V.reciprocal(p2, p1))
                step(V.tensor_tensor(w_mix[:, 0, :], gw, p2, ALU.mult))
                step(V.tensor_tensor(w_mix[:, 1, :], w_mix[:, 0, :], w_mix[:, 1, :], ALU.mult))
                dve.wait_ge(r.placed, v + 1)
                pos = grid(5)
                step(V.tensor_copy(pos, ps[:, 5, 0:T * NE].rearrange("p (t e) -> p t e", t=T)))
                step(V.tensor_reduce(gsum[:, 0:1], ps[:, 6, 0:NE], AX.X, ALU.max))
                V.tensor_copy(count_i[:, int(s[3]), 0:NE], ps[:, 6, 0:NE])
                V.tensor_copy(count_i[:, int(s[3]), NE:NE + 1], gsum[:, 0:1])
                for j, (hot, p) in enumerate(((hot1, p1), (hot2, p2))):
                    step(V.tensor_tensor(grid(6), hot, pos, ALU.mult))
                    step(V.tensor_reduce(p, grid(6), AX.X, ALU.add))
                    vals = values[:, j * T:(j + 1) * T, :]
                    V.tensor_tensor(vals[:, :, 0:NE], hot, over(value[:, j, :], NE), ALU.mult)
                    step(V.tensor_tensor(vals[:, :, NE:2 * NE], hot, over(value[:, 2, :], NE), ALU.mult))
                slot_rows().then_inc(r.slots, 1)
                dve.wait_ge(r.tables_psum, v + 1)
                slot_indices(step).then_inc(r.tables, 1)
                dve.wait_ge(r.tables, v + 1)
                dve.wait_ge(r.h_stored, 16 * T * (v + 1))

            def index(s, i, b):
                if not isinstance(i, int) or i + moe_turn[s] > 0:
                    dve.wait_ge(gathered[b], i * 16 + 16 * PER * moe_turn[s])
                V.tensor_copy(now_g[:, b:b + 1], tab_u[:, 1, bass.ds(i * 2 + b, 1)]).then_inc(m.index, 1)

            def slot_cols(s, b, q):
                return V.tensor_tensor(xgT[:, b, :].rearrange("p (c s) -> p c s", c=KC)[:, 4 * q:4 * q + 4, :],
                                       ps[:, q, 0:4 * SLOTS].rearrange("p (a s) -> p a s", a=4),
                                       over(gcols[:, gain_no[s], 4 * q:4 * q + 4], SLOTS), ALU.mult)

            def columns(s, i, b):
                n = 2 * i + (b + NE * moe_turn[s])
                for q in range(2):
                    dve.wait_ge(m.x_turned, 2 * n + (q + 1))
                    slot_cols(s, b, q).then_inc(m.x_cols, 1)

            def expert(s, i, b, has_next=True, has_after=True):
                v, k = moe_turn[s], first[s] + 3 * b
                n = 2 * i + (b + NE * v)
                dve.wait_ge(m.silu, n + 1)
                dve.wait_ge(al.chunk_used, i * RING + k + 2)
                V.tensor_tensor(hid[:, b, :], sg[:, b, :], ps[SLOTS:2 * SLOTS, 3, :], ALU.mult).then_inc(m.hidden, 1)
                if has_after:
                    index(s, i + 1, b)
                if has_next:
                    columns(s, i + b, 1 - b)
                if not isinstance(i, int) or i + v > 0:
                    dve.wait_ge(scattered[b], i * 16 + 16 * PER * v)
                V.tensor_copy(now_s[:, b:b + 1], tab_u[:, 0, bass.ds(i * 2 + b, 1)])
                dve.wait_ge(al.chunk_used, i * RING + k + 3)
                V.tensor_copy(yb[:, b, N:D], ps[SLOTS:2 * SLOTS, 6, :]).then_inc(m.y_right, 1)

            def moe(s):
                v = moe_turn[s]
                route(s)
                index(s, 0, 0)
                index(s, 0, 1)
                columns(s, 0, 0)
                for b in range(2):
                    expert(s, 0, b)
                with dve.Fori(1, PER - 1) as i:
                    for b in range(2):
                        expert(s, i, b)
                for b in range(2):
                    expert(s, PER - 1, b, has_next=(b == 0), has_after=False)
                over_blocks(s)
                x = as_tiles(place[s][0])
                for t in range(T):
                    dve.wait_ge(back[t], 16 * (v + 1))
                    for k in range(2):
                        last = V.scalar_tensor_tensor(out=x[:, t, :], in0=yc[:, t, k * D:(k + 1) * D],
                                                      scalar=w_mix[:, k, t:t + 1], in1=x[:, t, :],
                                                      op0=ALU.mult, op1=ALU.add)
                        if k == 0:
                            step(last)
                    last.then_inc(al.x_tiles, 1)

            def over_blocks(s):
                f = ov[int(s[3])]
                v = moe_turn[s]
                most = dve.value_load(count_i[0:1, int(s[3]), NE:NE + 1], min_val=0, max_val=S)
                inner = Order(dve, f.order)
                with dve.If(most > SLOTS):
                    for b in range(2):
                        dve.wait_ge(scattered[b], 16 * PER * (v + 1))
                    for b in range(1, SLOT_BLOCKS):
                        with dve.If(most > b * SLOTS):
                            inner(V.tensor_scalar(p1, p1, -float(SLOTS), None, ALU.add))
                            inner(V.tensor_scalar(p2, p2, -float(SLOTS), None, ALU.add))
                            slot_rows().then_inc(f.hot, 1)
                            dve.wait_ge(f.tab, b)
                            inner(slot_indices(inner))
                            with dve.Fori(0, NE) as q:
                                n = q + (b - 1) * NE
                                V.tensor_copy(now_g[:, 0:1], tab_u[:, 1, bass.ds(q, 1)])
                                V.tensor_copy(now_s[:, 0:1], tab_u[:, 0, bass.ds(q, 1)]).then_inc(f.dve, 1)
                                dve.wait_ge(f.pe, n * 4 + 1)
                                for h in range(2):
                                    last = slot_cols(s, 0, h)
                                last.then_inc(f.dve, 1)
                                dve.wait_ge(f.act, n + 1)
                                V.tensor_tensor(hid[:, 0, :], sg[:, 0, :], ps[SLOTS:2 * SLOTS, 3, :], ALU.mult).then_inc(f.dve, 1)
                                dve.wait_ge(f.pe, n * 4 + 3)
                                V.tensor_copy(hidT[:, 0, :], ps[:, 4, 0:FF // P * SLOTS]).then_inc(f.dve, 1)
                                dve.wait_ge(f.pe, n * 4 + 4)
                                V.tensor_copy(yb[:, 0, 0:N], ps[0:SLOTS, 5, :])
                                V.tensor_copy(yb[:, 0, N:D], ps[SLOTS:2 * SLOTS, 6, :]).then_inc(f.dve, 1)
                                dve.wait_ge(f.scatter, n * 16 + 16)
                                dve.sem_inc(f.dve, 1)

            for s in stages:
                norm(s)
                if s == "even":
                    even()
                elif s == "odd":
                    odd_dve(dve, step, add_mixed)
                else:
                    moe(s)

        @block.gpsimd
        def _(pool):
            pool.memset(ones[:, :], 1.0).then_inc(al.const, 16)
            last_row, last_assignment = pool.to_reg(S - 1), pool.to_reg(2 * S - 1)

            def gather(s, i, b):
                L, v = int(s[3]), moe_turn[s]
                n = 2 * i + (b + NE * v)
                pool.wait_ge(m.index, n + 1)
                if not isinstance(n, int) or n >= 2:
                    pool.wait_ge(m.x_cols, 2 * n - 2)
                pool.sem_inc(al.passed, 1)
                pool.indirect_dma_start(xg[:, b, :], None, h_dram[L], bass.IndirectOffsetOnAxis(ap=now_g[:, b:b + 1], axis=0),
                                        bounds_check=last_row, oob_is_err=False).then_inc(gathered[b], 16)

            def scatter(s, i, b):
                L, v = int(s[3]), moe_turn[s]
                n = 2 * i + (b + NE * v)
                pool.wait_ge(m.y_left, n + 1)
                pool.wait_ge(m.y_right, n + 1)
                pool.sem_inc(al.passed, 1)
                pool.indirect_dma_start(y_dram[L], bass.IndirectOffsetOnAxis(ap=now_s[:, b:b + 1], axis=0), yb[:, b, :], None,
                                        bounds_check=last_assignment, oob_is_err=False).then_inc(scattered[b], 16)

            def moe(s):
                v, L = moe_turn[s], int(s[3])
                f = ov[L]
                pool.wait_ge(r.h_stored, 16 * T * (v + 1))
                gather(s, 0, 0)
                gather(s, 0, 1)
                for b in range(2):
                    gather(s, 1, b)
                    scatter(s, 0, b)
                with pool.Fori(1, PER - 1) as i:
                    for b in range(2):
                        gather(s, i + 1, b)
                        scatter(s, i, b)
                for b in range(2):
                    scatter(s, PER - 1, b)
                most = pool.value_load(count_i[0:1, int(s[3]), NE:NE + 1], min_val=0, max_val=S)
                with pool.If(most > SLOTS):
                    for b in range(1, SLOT_BLOCKS):
                        with pool.If(most > b * SLOTS), pool.Fori(0, NE) as q:
                            n = q + (b - 1) * NE
                            pool.wait_ge(f.dve, n * 6 + 1)
                            pool.sem_inc(al.passed, 1)
                            pool.indirect_dma_start(xg[:, 0, :], None, h_dram[L],
                                                    bass.IndirectOffsetOnAxis(ap=now_g[:, 0:1], axis=0),
                                                    bounds_check=last_row, oob_is_err=False).then_inc(f.gather, 16)
                            pool.wait_ge(f.dve, n * 6 + 5)
                            pool.sem_inc(al.passed, 1)
                            pool.indirect_dma_start(y_dram[L], bass.IndirectOffsetOnAxis(ap=now_s[:, 0:1], axis=0),
                                                    yb[:, 0, :], None,
                                                    bounds_check=last_assignment, oob_is_err=False).then_inc(f.scatter, 16)
                            pool.wait_ge(f.scatter, n * 16 + 16)
                            pool.sem_inc(al.passed, 1)

            for s in stages:
                if s[:3] == "moe":
                    moe(s)

    return nc


def kernel(**inputs):
    import numpy as _np
    import concourse.bacc as _bacc
    from concourse import mybir as _mybir
    from concourse.bass_utils import run_bass_kernel_spmd as _run

    nc = _bacc.Bacc("TRN2", target_bir_lowering=False, num_devices=1)
    arrays, io = {}, {}
    for name, a in list(inputs.items()) + list(constants().items()):
        a = _np.ascontiguousarray(a)
        arrays[f"in_{name}_dram"] = a
        io[name] = nc.dram_tensor(f"in_{name}_dram", a.shape, _mybir.dt.from_np(a.dtype), kind="ExternalInput").ap()
    out = nc.dram_tensor("out_0_dram", (1, S, D), _mybir.dt.from_np(_np.dtype("float32")), kind="ExternalOutput").ap()
    build(nc, io, out, STAGES)
    r = _run(nc, [arrays], core_ids=[0])
    return r.results[0]["out_0_dram"]
```
